# Optimizing a Trainium2 kernel written in Bass

```python
import math
import jax, jax.numpy as jnp
from jax import lax
import numpy as np

D_MODEL = 1024
BATCH = 1
SEQ = 256
DEPTH = 2
DEC_BATCH = 8
DEC_SEQ = 8
PAST_LEN = 2048
PAGE_SIZE = 128

MIX_WIDTH = D_MODEL
HG_WIDTH = MIX_WIDTH // 2
HG_DV = 128
HG_HEADS = HG_WIDTH // HG_DV
HG_DK = 128
HG_FDIM = HG_HEADS * HG_DK
HG_CHUNK = 64
SSD_WIDTH = MIX_WIDTH - HG_WIDTH
SSD_HEADDIM = 64
SSD_HEADS = SSD_WIDTH // SSD_HEADDIM
SSD_GROUPS = 2
SSD_HPG = SSD_HEADS // SSD_GROUPS
SSD_STATE = 128
SSD_CHUNK = 128
CONV_WIDTH = 4
CONV_DIM = SSD_WIDTH + 2 * SSD_GROUPS * SSD_STATE
SPLIT_SIZES = (HG_FDIM, HG_FDIM, HG_WIDTH, HG_WIDTH, SSD_WIDTH, CONV_DIM, SSD_HEADS)
SPLIT_IDX = tuple(int(v) for v in np.cumsum(SPLIT_SIZES)[:-1])
IN_PROJ_DIM = int(sum(SPLIT_SIZES))
D_FF = 2816
N_EXPERTS = 8
TOP_K = 2
D_FF_EXPERT = 3584
N_DENSE = (DEPTH + 1) // 2
N_MOE = DEPTH // 2
EPS = 1e-6

kernel_name = "hymba_style_hgrn2_ssd_decoder_step"

def rmsnorm(x, g):
    xf = x.astype(jnp.float32)
    y = xf * lax.rsqrt(jnp.mean(xf * xf, axis=-1, keepdims=True) + EPS)
    return (y * g.astype(jnp.float32)).astype(x.dtype)

def _to_chunks(a, c):
    bsz, L = a.shape[:2]
    n = -(-L // c)
    a = jnp.pad(a, [(0, 0), (0, n * c - L)] + [(0, 0)] * (a.ndim - 2))
    a = a.reshape((bsz, n, c) + a.shape[2:])
    return jnp.moveaxis(a, 1, 0)

def _from_chunks(a, L):
    a = jnp.moveaxis(a, 0, 1)
    bsz, n, c = a.shape[:3]
    return a.reshape((bsz, n * c) + a.shape[3:])[:, :L]

def hgrn2_chunked(q, k, v, logf, s0):
    L = q.shape[1]
    c = min(HG_CHUNK, L)
    causal = jnp.tril(jnp.ones((c, c), dtype=bool))[None, :, :, None, None]
    xs = tuple(_to_chunks(t.astype(jnp.float32), c) for t in (q, k, v, logf))

    def step(s, inp):
        qb, kb, vb, gb = inp
        G = jnp.cumsum(gb, axis=1)
        o_inter = jnp.einsum('bthk,bhkv->bthv', qb * jnp.exp(G), s)
        diff = G[:, :, None] - G[:, None, :]
        decay = jnp.exp(jnp.where(causal, diff, -jnp.inf))
        scores = jnp.einsum('bthk,btshk->btsh', qb, decay * kb[:, None])
        o_intra = jnp.einsum('btsh,bshv->bthv', scores, vb)
        g_last = G[:, -1]
        k_dec = kb * jnp.exp(g_last[:, None] - G)
        s_new = jnp.exp(g_last)[..., None] * s + jnp.einsum('bshk,bshv->bhkv', k_dec, vb)
        return s_new, o_inter + o_intra

    s_fin, o = lax.scan(step, s0.astype(jnp.float32), xs)
    return _from_chunks(o, L), s_fin

def ssd_chunked(xdt, a, bm, cm, h0):
    bsz, L = xdt.shape[:2]
    c = min(SSD_CHUNK, L)
    causal = jnp.tril(jnp.ones((c, c), dtype=bool))[None, :, :, None, None]
    xs = tuple(_to_chunks(t.astype(jnp.float32), c) for t in (xdt, a, bm, cm))

    def step(h, inp):
        xb, ab, bb, cb = inp
        xg = xb.reshape(bsz, c, SSD_GROUPS, SSD_HPG, SSD_HEADDIM)
        acum = jnp.cumsum(ab, axis=1).reshape(bsz, c, SSD_GROUPS, SSD_HPG)
        hg = h.reshape(bsz, SSD_GROUPS, SSD_HPG, SSD_STATE, SSD_HEADDIM)
        y_inter = jnp.einsum('btgn,bgrnp->btgrp', cb, hg) * jnp.exp(acum)[..., None]
        diff = acum[:, :, None] - acum[:, None, :]
        decay = jnp.exp(jnp.where(causal, diff, -jnp.inf))
        cb_bs = jnp.einsum('btgn,bsgn->btsg', cb, bb)
        y_intra = jnp.einsum('btsgr,bsgrp->btgrp', cb_bs[..., None] * decay, xg)
        a_last = acum[:, -1]
        w = jnp.exp(a_last[:, None] - acum)
        h_new = jnp.exp(a_last)[..., None, None] * hg + jnp.einsum('bsgn,bsgrp->bgrnp', bb, xg * w[..., None])
        return h_new.reshape(h.shape), (y_inter + y_intra).reshape(bsz, c, SSD_HEADS, SSD_HEADDIM)

    h_fin, y = lax.scan(step, h0.astype(jnp.float32), xs)
    return _from_chunks(y, L), h_fin

def parallel_mixer(hn, lb, w_in, conv_w, conv_b, a_log, dt_bias, d_skip, hg_norm, ssd_norm, w_out,
                   s_hg, s_ssd, conv_buf):
    bsz, L, _ = hn.shape
    dtype = hn.dtype
    proj = jnp.einsum('bld,de->ble', hn, w_in)
    q, f, i, og, z, xbc, dt = jnp.split(proj, SPLIT_IDX, axis=-1)

    q = jax.nn.silu(q).reshape(bsz, L, HG_HEADS, HG_DK)
    fz = f.astype(jnp.float32)
    lbf = lb.astype(jnp.float32)
    log_f = jnp.logaddexp(jnp.log(lbf), jnp.log1p(-lbf) + jax.nn.log_sigmoid(fz))
    k_in = (1.0 - lbf) * jax.nn.sigmoid(-fz)
    log_f = log_f.reshape(bsz, L, HG_HEADS, HG_DK)
    k_in = k_in.reshape(bsz, L, HG_HEADS, HG_DK)
    v = i.reshape(bsz, L, HG_HEADS, HG_DV)
    o_hg, s_hg_new = hgrn2_chunked(q, k_in, v, log_f, s_hg)
    o_hg = rmsnorm(o_hg, hg_norm.reshape(HG_HEADS, HG_DV)).reshape(bsz, L, HG_WIDTH)
    o_hg = (o_hg * jax.nn.silu(og.astype(jnp.float32))).astype(dtype)

    xpad = jnp.concatenate([conv_buf.astype(dtype), xbc], axis=1)
    conv = conv_b[None, None, :]
    for tap in range(CONV_WIDTH):
        conv = conv + conv_w[tap][None, None, :] * xpad[:, tap:tap + L]
    conv = jax.nn.silu(conv)
    conv_buf_new = xpad[:, xpad.shape[1] - (CONV_WIDTH - 1):]
    xs, bm, cm = jnp.split(conv, (SSD_WIDTH, SSD_WIDTH + SSD_GROUPS * SSD_STATE), axis=-1)
    xs = xs.reshape(bsz, L, SSD_HEADS, SSD_HEADDIM)
    bm = bm.reshape(bsz, L, SSD_GROUPS, SSD_STATE)
    cm = cm.reshape(bsz, L, SSD_GROUPS, SSD_STATE)
    dtf = jax.nn.softplus(dt.astype(jnp.float32) + dt_bias.astype(jnp.float32))
    A = -jnp.exp(a_log.astype(jnp.float32))
    xf = xs.astype(jnp.float32)
    y, s_ssd_new = ssd_chunked(xf * dtf[..., None], dtf * A, bm, cm, s_ssd)
    y = y + d_skip.astype(jnp.float32)[:, None] * xf
    y = y.reshape(bsz, L, SSD_WIDTH) * jax.nn.silu(z.astype(jnp.float32))
    y = rmsnorm(y.reshape(bsz, L, SSD_GROUPS, SSD_WIDTH // SSD_GROUPS),
                ssd_norm.reshape(SSD_GROUPS, SSD_WIDTH // SSD_GROUPS)).reshape(bsz, L, SSD_WIDTH)

    mixed = jnp.concatenate([o_hg, y.astype(dtype)], axis=-1)
    out = jnp.einsum('ble,ed->bld', mixed, w_out)
    return out, s_hg_new, s_ssd_new, conv_buf_new

def swiglu(h, w_in, w_out):
    g, u = jnp.split(jnp.einsum('bld,df->blf', h, w_in), 2, axis=-1)
    return jnp.einsum('blf,fd->bld', jax.nn.silu(g) * u, w_out)

def moe_swiglu(h, w_router, w_exp_in, w_exp_out):
    logits = jnp.einsum('bld,de->ble', h, w_router).astype(jnp.float32)
    top_v, top_i = lax.top_k(logits, TOP_K)
    gates = jax.nn.softmax(top_v, axis=-1)
    dense_gate = jnp.sum(jax.nn.one_hot(top_i, N_EXPERTS, dtype=jnp.float32) * gates[..., None], axis=-2)
    dense_gate = dense_gate.astype(h.dtype)
    y = jnp.zeros_like(h)
    for e in range(N_EXPERTS):
        y = y + dense_gate[..., e:e + 1] * swiglu(h, w_exp_in[e], w_exp_out[e])
    return y

def trunk(x, s_hg, s_ssd, conv_buf, norm_mix, w_in, conv_w, conv_b, a_log, dt_bias, d_skip,
          lb_param, hg_norm, ssd_norm, w_out, norm_ffn, w_ffn_in, w_ffn_out, w_router,
          w_exp_in, w_exp_out, norm_final):
    lb_p = jax.nn.softmax(lb_param.astype(jnp.float32), axis=0)
    h = x
    new_hg, new_ssd, new_conv = [], [], []
    for l in range(DEPTH):
        lb = jnp.sum(lb_p[1:l + 1], axis=0)
        mix, sh, ss, cb = parallel_mixer(rmsnorm(h, norm_mix[l]), lb, w_in[l], conv_w[l], conv_b[l],
                                         a_log[l], dt_bias[l], d_skip[l], hg_norm[l], ssd_norm[l],
                                         w_out[l], s_hg[l], s_ssd[l], conv_buf[l])
        h = h + mix
        hn = rmsnorm(h, norm_ffn[l])
        if l % 2 == 0:
            h = h + swiglu(hn, w_ffn_in[l // 2], w_ffn_out[l // 2])
        else:
            h = h + moe_swiglu(hn, w_router[l // 2], w_exp_in[l // 2], w_exp_out[l // 2])
        new_hg.append(sh.astype(s_hg.dtype))
        new_ssd.append(ss.astype(s_ssd.dtype))
        new_conv.append(cb.astype(conv_buf.dtype))
    return rmsnorm(h, norm_final), jnp.stack(new_hg), jnp.stack(new_ssd), jnp.stack(new_conv)

def setup_inputs(seed: int = 0) -> dict:
    key = jax.random.key(seed)
    ks = jax.random.split(key, 24)
    f32 = jnp.float32
    nrm = lambda k, shape, s: jax.random.normal(k, shape, f32) * s
    dt0 = jnp.exp(jax.random.uniform(ks[9], (DEPTH, SSD_HEADS), f32, math.log(1e-3), math.log(1e-1)))
    return {
        "x_prompt": nrm(ks[0], (BATCH, SEQ, D_MODEL), 1.0),
        "x_sample": nrm(ks[1], (DEC_BATCH, DEC_SEQ, D_MODEL), 1.0),
        "state_hgrn": nrm(ks[2], (DEPTH, DEC_BATCH, HG_HEADS, HG_DK, HG_DV), 0.5),
        "state_ssm": nrm(ks[3], (DEPTH, DEC_BATCH, SSD_HEADS, SSD_STATE, SSD_HEADDIM), 0.1),
        "state_conv": nrm(ks[4], (DEPTH, DEC_BATCH, CONV_WIDTH - 1, CONV_DIM), 1.0),
        "norm_mix": 1.0 + nrm(ks[5], (DEPTH, D_MODEL), 0.01),
        "w_in": nrm(ks[6], (DEPTH, D_MODEL, IN_PROJ_DIM), D_MODEL ** -0.5),
        "conv_w": nrm(ks[7], (DEPTH, CONV_WIDTH, CONV_DIM), CONV_WIDTH ** -0.5),
        "conv_b": nrm(ks[8], (DEPTH, CONV_DIM), 0.01),
        "a_log": jnp.log(jax.random.uniform(ks[10], (DEPTH, SSD_HEADS), f32, 1.0, 16.0)),
        "dt_bias": dt0 + jnp.log(-jnp.expm1(-dt0)),
        "d_skip": 1.0 + nrm(ks[11], (DEPTH, SSD_HEADS), 0.01),
        "lb_param": nrm(ks[12], (DEPTH, HG_FDIM), 0.1),
        "hg_norm": 1.0 + nrm(ks[13], (DEPTH, HG_WIDTH), 0.01),
        "ssd_norm": 1.0 + nrm(ks[14], (DEPTH, SSD_WIDTH), 0.01),
        "w_out": nrm(ks[15], (DEPTH, MIX_WIDTH, D_MODEL), MIX_WIDTH ** -0.5),
        "norm_ffn": 1.0 + nrm(ks[16], (DEPTH, D_MODEL), 0.01),
        "w_ffn_in": nrm(ks[17], (N_DENSE, D_MODEL, 2 * D_FF), D_MODEL ** -0.5),
        "w_ffn_out": nrm(ks[18], (N_DENSE, D_FF, D_MODEL), D_FF ** -0.5),
        "w_router": nrm(ks[19], (N_MOE, D_MODEL, N_EXPERTS), D_MODEL ** -0.5),
        "w_exp_in": nrm(ks[20], (N_MOE, N_EXPERTS, D_MODEL, 2 * D_FF_EXPERT), D_MODEL ** -0.5),
        "w_exp_out": nrm(ks[21], (N_MOE, N_EXPERTS, D_FF_EXPERT, D_MODEL), D_FF_EXPERT ** -0.5),
        "norm_final": 1.0 + nrm(ks[22], (D_MODEL,), 0.01),
    }

def reference(x_prompt, x_sample, state_hgrn, state_ssm, state_conv, norm_mix, w_in, conv_w, conv_b,
              a_log, dt_bias, d_skip, lb_param, hg_norm, ssd_norm, w_out, norm_ffn, w_ffn_in,
              w_ffn_out, w_router, w_exp_in, w_exp_out, norm_final):
    weights = (norm_mix, w_in, conv_w, conv_b, a_log, dt_bias, d_skip, lb_param, hg_norm, ssd_norm,
               w_out, norm_ffn, w_ffn_in, w_ffn_out, w_router, w_exp_in, w_exp_out, norm_final)
    hg0 = jnp.zeros((DEPTH, BATCH) + state_hgrn.shape[2:], state_hgrn.dtype)
    ssm0 = jnp.zeros((DEPTH, BATCH) + state_ssm.shape[2:], state_ssm.dtype)
    conv0 = jnp.zeros((DEPTH, BATCH) + state_conv.shape[2:], state_conv.dtype)
    y_prompt, hg_p, ssm_p, conv_p = trunk(x_prompt, hg0, ssm0, conv0, *weights)
    y_sample, hg_s, ssm_s, conv_s = trunk(x_sample, state_hgrn, state_ssm, state_conv, *weights)
    return (y_prompt, y_sample, hg_p, ssm_p, conv_p, hg_s, ssm_s, conv_s)


_drawn_inputs = setup_inputs


def setup_inputs(seed=0):
    import zlib

    import numpy as np

    out = dict(_drawn_inputs(seed))
    spreads = {}
    factors = {'d_skip': 36.088,
     'hg_norm': 5.429,
     'norm_ffn': 2.816,
     'norm_final': 31.833,
     'conv_b': 2.878,
     'ssd_norm': 8.0}
    for name, (base, spread) in spreads.items():
        noise = np.random.default_rng([zlib.crc32(name.encode()), seed]).standard_normal(out[name].shape)
        drawn = base * np.exp(spread * noise) if base else spread * noise
        out[name] = __import__('jax').numpy.asarray(drawn.astype(out[name].dtype))
    for name, factor in factors.items():
        out[name] = (out[name] * factor).astype(out[name].dtype)
    return out
```

```python
from contextlib import ExitStack

import numpy as np

import concourse.bass as bass
from concourse import mybir

F32 = mybir.dt.float32
F32R = mybir.dt.float32r
I32 = mybir.dt.int32
ACT = mybir.ActivationFunctionType
ALU = mybir.AluOpType
AX = mybir.AxisListType

P = 128
D = 1024
KT = D // P
NPR, NSQ, LSQ = 256, 8, 8
NS = NSQ * LSQ
TOK = NPR + NS
TILES = [(0, 128), (128, 128), (256, 64)]
DEPTH = 2
H = 4
NH, HD, G = 8, 64, 2
CONV = 1024
TAPS = 4
PADC = (TAPS - 1) + NPR + NSQ * (TAPS - 1 + LSQ)
NIN = 3592
DFF, DFE, NE = 2816, 3584, 8
EPS = 1e-6
CAP = 128
MAXR = -(-TOK // CAP)

LV = 7
LS = 3
RING = 6
UN = 2048


def level_tables(n, levels, seq):
    i = np.arange(n)
    same = (i[:, None] // seq) == (i[None, :] // seq)
    w = np.zeros((n, levels + 1, n), np.float32)
    m = np.zeros((n, levels + 1, n), np.float32)
    for v in range(levels):
        b = 1 << v
        for t in range(n):
            ref = (t // (2 * b)) * 2 * b + b - 1
            if t > ref:
                w[ref + 1:t + 1, v, t] = 1
            else:
                w[t + 1:ref + 1, v, t] = 1
        left = (i // b) % 2 == 0
        pair = (i[:, None] // (2 * b)) == (i[None, :] // (2 * b))
        m[:, v, :] = pair & left[:, None] & ~left[None, :]
    w[:, levels, :] = same & (i[:, None] <= i[None, :])
    m[:, levels, :] = np.eye(n)
    after = (same & (i[:, None] > i[None, :])).astype(np.float32)
    return w, after, m


def constants():
    wp, lp, mp = level_tables(128, LV, 128)
    ws, ls, ms = level_tables(NS, LS, LSQ)
    i = np.arange(P)
    seq = ((i[:, None] // LSQ) == np.arange(NSQ)[None, :]).astype(np.float32)
    lspad = np.zeros((NS, P), np.float32)
    lspad[:, :NS] = ls
    parts = {
        "w": wp.reshape(P, -1), "l": lp, "ws": ws.reshape(NS, -1), "ls": lspad, "ones": np.ones((P, P)),
        "mask": mp.reshape(P, -1), "id": np.eye(P), "ms": ms.reshape(NS, -1), "seq": seq,
        "iota": np.tile(i[None, :], (P, 1)), "before": (i[:, None] < i[None, :]),
    }
    at, n = {}, 0
    for k, v in parts.items():
        at[k] = (n, v.shape[1])
        n += v.shape[1]
    out = np.zeros((P, n), np.float32)
    for k, v in parts.items():
        out[:v.shape[0], at[k][0]:at[k][0] + v.shape[1]] = v
    return out, at


def unit_plan():
    u, plan = 0, {}
    for l in range(DEPTH):
        plan["in", l] = u
        u += 14
        plan["out", l] = u
        u += 4
        if l % 2 == 0:
            plan["up", l] = u
            u += 22
            plan["down", l] = u
            u += 16
        else:
            plan["moe", l] = u
    return plan


PLAN = unit_plan()
CHUNKS = [2560, 3072, 0, 1536, 2048, 512, 1024]
C_XS, C_BC, C_Q, C_OG, C_Z, C_F, C_I = range(7)
EC = DFE // 512
EXPERT_UNITS = [("up", 0, i) for i in range(4)]
for _c in range(1, EC):
    EXPERT_UNITS += [("up", _c, i) for i in range(4)] + [("down", _c - 1, i) for i in range(2)]
EXPERT_UNITS += [("down", EC - 1, i) for i in range(2)]
EU = len(EXPERT_UNITS)
AHEAD = 3
ERING = 7
assert EU % AHEAD == 0 and EU % ERING == 0
UP_LAST = [EXPERT_UNITS.index(("up", c, 3)) for c in range(EC)]
TURN_AT = [EXPERT_UNITS.index(("up", c + 1, 1)) for c in range(EC - 1)] + [EXPERT_UNITS.index(("down", EC - 2, 1))]


def build(nc, a, outs, table, at):
    y_prompt, y_sample, hg_p, ssm_p, conv_p, hg_s, ssm_s, conv_s = outs
    ctx = ExitStack()
    with ctx:
        base = nc.sbuf_base
        room = nc.sbuf_usable_end - base - 64
        base = -(-base // 64) * 64
        fence = ctx.enter_context(nc.sbuf_tensor("fence", [P, (room - 64) // 4], F32))
        cursor = [base]

        def put(name, shape, dt=F32, offset=None):
            size = 4 * int(np.prod(shape[1:]))
            if offset is None:
                offset = cursor[0]
                cursor[0] = offset + -(-size // 32) * 32
                assert cursor[0] <= base + room - 128, (name, cursor[0] - base, room)
            return nc.alloc_sbuf_tensor_at(name, shape, dt, offset=offset)

        xT = put("xT", [P, KT, TOK])
        hnH = put("hnH", [P, KT, TOK], F32R)
        hnL = put("hnL", [P, KT, TOK], F32R)
        ring = put("ring", [P, RING, UN])
        spH = put("spH", [P, 2, UN], F32R)
        spL = put("spL", [P, 2, UN], F32R)
        nr = at["mask"][0]
        tabR = put("tabR", [P, nr], F32R)
        tab = put("tab", [P, table.shape[1] - nr])
        vec = put("vec", [P, DEPTH, 68])
        wdt = put("wdt", [P, DEPTH, KT, NH])
        wro = put("wro", [P, KT, NE])
        bc = put("bc", [P, DEPTH, 3, NH])
        eps = put("eps", [P, 1])
        lbom = put("lbom", [P, DEPTH, 2, H])
        lbt = put("lbt", [P, 4, H])
        arena = cursor[0]

        def tabv(name, dt=F32):
            o, n = at[name]
            if o < nr:
                v = tabR[:, o:o + n]
                return v if dt == F32R else v.bitcast(F32)
            return tab[:, o - nr:o - nr + n]

        ident = tabv("id")
        onesf = tabv("ones")

        cursor[0] = arena
        qT = put("qT", [P, H, TOK])
        kT = put("kT", [P, H, TOK])
        lfT = put("lfT", [P, H, TOK])
        oT = put("oT", [P, H, TOK])
        ogT = put("ogT", [P, H, TOK])
        zT = put("zT", [P, H, TOK])
        cvT = put("cvT", [P, 8, TOK])
        tok0 = cursor[0]
        lfH = put("lfH", [P, H * P], F32R)
        lfL = put("lfL", [P, H * P], F32R)
        kd = put("kd", [P, H * P])
        vtk = put("vtk", [P, H * P])
        xdt = put("xdt", [P, NH * HD])
        xw = put("xw", [P, NH * HD])
        Bt = put("Bt", [P, G * P])
        SH = put("SH", [P, H * P])
        rstd = put("rstd", [P, TOK], offset=cursor[0] - 4 * H * P)
        SS = put("SS", [P, NH * HD])
        slab = put("slab", [P, 4, 512])
        ov = cursor[0]
        M = put("M", [P, LV + 1, P])
        Yq = put("Yq", [P, LV + 1, P])
        Yk = put("Yk", [P, LV, P])
        sc0 = cursor[0]
        SC = put("SC", [P, LV + 1, P])
        qG = put("qG", [P, H, NS])
        egl = put("egl", [P, H, NSQ])
        dtb = put("dtb", [P, 5, 3, NH])
        wsm = put("wsm", [P, NH])
        ea = put("ea", [P, NSQ * NH])
        am = put("am", [P, NSQ, NH])
        xbc = put("xbc", [P, 8, PADC], offset=ov)
        cvt = put("cvt", [P, 2, PADC], offset=sc0)
        cst = put("cst", [NSQ * 3, CONV], offset=tok0)
        cpk = put("cpk", [P, 8, 3 + NSQ * 3], offset=tok0 + 4 * CONV)
        cso = put("cso", [3 + NSQ * 3, CONV], offset=tok0 + 8 * CONV)
        kdm = put("kdm", [NS, 2, H * P], offset=tok0 + 4 * 4 * H * P)
        Bm = put("Bm", [NS, 2, G * P], offset=tok0 + 2 * 4 * H * P)
        La = put("La", [P, NH, P], offset=ov + 4 * 1024)
        t1 = put("t1", [P, 4, P], offset=ov + 8 * 1024)
        CBm = put("CBm", [P, G, P], offset=tok0)
        aex = put("aex", [P, NH, HD], offset=sc0)
        EE = put("EE", [P, 4, P], offset=sc0 + 4 * 512)
        sq = put("sq", [P, KT, TOK], offset=arena)
        xin = put("xin", [P, 3, D], offset=arena + 4 * KT * TOK)
        vin = put("vin", [68, DEPTH, P], offset=arena + 4 * (KT * TOK + 3 * D))
        sqh = put("sqh", [P, H, TOK], offset=arena)
        sqs = put("sqs", [P, 4, TOK], offset=arena + 4 * H * TOK)
        rsh = put("rsh", [P, H, TOK], offset=arena + 8 * H * TOK)
        rss = put("rss", [P, G, TOK], offset=ov)
        stage = put("stage", [P, nr], offset=tok0)

        NF = DFF // P
        cursor[0] = arena + 4 * KT * TOK
        hfH = put("hfH", [P, NF, TOK], F32R)
        hfL = put("hfL", [P, NF, TOK], F32R)
        gs = put("gs", [P, 2, TOK])
        hf = put("hf", [P, 2, TOK])

        cursor[0] = arena
        hkH = put("hkH", [P, 3, D], F32R)
        hkL = put("hkL", [P, 3, D], F32R)
        ht = put("ht", [P, 3, D])
        yH = put("yH", [P, D], F32R)
        yL = put("yL", [P, D], F32R)
        sg = put("sg", [P, 2, 512])
        hTH = put("hTH", [P, 4, P], F32R)
        hTL = put("hTL", [P, 4, P], F32R)
        sel = put("sel", [P, 3, P], F32R)
        selT = put("selT", [P, 3, P], F32R)
        sml = put("sml", [P, 12, 3, NE])
        rank = put("rank", [P, NE + 1, 3])
        gate = put("gate", [P, NE, 3])
        rk = put("rk", [P, 2, 3])
        rnd = put("rnd", [P, 4])
        rndi = put("rndi", [P, 1], I32)
        ring6 = put("ring6", [P, 1, UN])
        spH2 = put("spH2", [P, 1, UN], F32R)
        spL2 = put("spL2", [P, 1, UN], F32R)
        sqm = put("sqm", [P, KT, TOK], offset=arena + 4 * 9 * D)
        gfin = put("gfin", [P, D], offset=arena)
        fsq = put("fsq", [P, 3, D], offset=arena + 4 * 3 * D)
        fss = put("fss", [P, 4], offset=arena + 4 * D)
        XH = put("XH", [P, KT, P], F32R, offset=base + 4 * KT * TOK)
        XL = put("XL", [P, KT, P], F32R, offset=base + 8 * KT * TOK)

        ps = ctx.enter_context(nc.psum_tensor("ps", [P, 8, 512], F32))

        sems = {}

        def S(name):
            if name not in sems:
                sems[name] = ctx.enter_context(nc.semaphore(name))
            return sems[name]

        landed = [S(f"landed{i}") for i in range(RING + 1)]
        slab_in = [S(f"slab_in{i}") for i in range(4)]
        slab_out = [S(f"slab_out{i}") for i in range(4)]

        U0 = PLAN["moe", 1]

        def eslot(j):
            i = j % ERING
            if i == ERING - 1:
                return ring6[:, 0], landed[RING], 0
            q = (U0 + i) % RING
            return ring[:, q], landed[q], len(range(q, U0, RING))

        def esplit(j):
            i = j % AHEAD
            return (spH2[:, 0], spL2[:, 0]) if i == 2 else (spH[:, i], spL[:, i])

        def raw(u, n=UN):
            return ring[:, u % RING, 0:n]

        def unit_src(u):
            for l in range(DEPTH):
                i = u - PLAN["in", l]
                if 0 <= i < 14:
                    c, h = divmod(i, 2)
                    src = a["w_in"][l, h * 512:(h + 1) * 512, CHUNKS[c]:CHUNKS[c] + 512]
                    return src.rearrange("(k p) n -> p k n", p=P), UN, 4
                i = u - PLAN["out", l]
                if 0 <= i < 4:
                    c, h = divmod(i, 2)
                    src = a["w_out"][l, h * 512:(h + 1) * 512, c * 512:(c + 1) * 512]
                    return src.rearrange("(k p) n -> p k n", p=P), UN, 4
            i = u - PLAN["up", 0]
            if 0 <= i < 22:
                j, h = divmod(i, 2)
                c0 = h * DFF + j * 256
                return a["w_ffn_in"][0, :, c0:c0 + 256].rearrange("(k p) n -> p k n", p=P), UN, 8
            i = u - PLAN["down", 0]
            m, h = divmod(i, 2)
            src = a["w_ffn_out"][0, h * 1408:(h + 1) * 1408, m * P:(m + 1) * P]
            return src.rearrange("(k p) n -> p k n", p=P), 1408, 11

        def LT(l, t):
            return l * 3 + t

        def LTH(l, t, h):
            return (l * 3 + t) * H + h

        block = ctx.enter_context(nc.Block())

        @block.sync
        def _(sp):
            for t, (o, n) in enumerate(TILES):
                src = a["x_prompt"][0, o:o + n] if t < 2 else a["x_sample"].rearrange("b s d -> (b s) d")
                sp.dma_start(xin[0:n, t], src).then_inc(S("x_in"), 16)
            for u in range(PLAN["moe", 1]):
                src, n, k = unit_src(u)
                if u >= RING:
                    sp.wait_ge(S("split_done"), u - RING + 1)
                dst = raw(u, n).rearrange("p (k n) -> p k n", k=k)
                sp.dma_start(dst, src).then_inc(landed[u % RING], 16)

            w1, w2 = a["w_exp_in"][0], a["w_exp_out"][0]

            def expert_load(e, it, j):
                kind, c, i = EXPERT_UNITS[j % EU]
                dst, sem, _ = eslot(j)
                if kind == "up":
                    c0 = (i // 2) * DFE + c * 512
                    src, k = w1[bass.ds(e, 1), (i % 2) * 512:(i % 2) * 512 + 512, c0:c0 + 512], 4
                else:
                    row = c * 512 + i * 256
                    src, k = w2[bass.ds(e, 1), row:row + 256, :], 2
                sp.wait_ge(S("split_done"), it * EU + (U0 + j - ERING + 1))
                sp.dma_start(dst.rearrange("p (k n) -> p k n", k=k),
                             src.rearrange("e (k p) n -> p (e k) n", p=P)).then_inc(sem, 16)

            def expert_loads(e, it):
                now = sp.snap(e)
                then = sp.snap((e + 1) % NE)
                for j in range(AHEAD, EU + AHEAD):
                    expert_load(now if j < EU else then, it, j)

            sp.wait_ge(S("split_done"), U0)
            for j in range(AHEAD):
                expert_load(0, 0, j)
            sp.wait_ge(S("out_evac"), 2 * DEPTH)
            sp.wait_ge(S("mixer_stored"), DEPTH)
            with sp.Fori(0, NE) as e:
                expert_loads(e, e)
            sp.wait_ge(S("rounds_ready"), 1)
            rounds = sp.value_load(rndi[0:1, 0:1], min_val=1, max_val=MAXR)
            with sp.If(rounds > 1):
                with sp.Fori(1, rounds) as r:
                    with sp.Fori(0, NE) as e:
                        expert_loads(e, sp.snap(r * NE + e))
        @block.gpsimd
        def _(pool):
            nc.gpsimd.memset(eps[:], EPS).then_inc(S("eps_set"), 1)
            pool.dma_start(tab[:], a["table"][:, nr:]).then_inc(S("tab_in"), 16)
            pool.dma_start(stage[:], a["table"][:, 0:nr]).then_inc(S("stage_in"), 16)
            for l in range(DEPTH):
                r = 0
                for src, k in ((a["norm_mix"][l], 8), (a["norm_ffn"][l], 8), (a["conv_b"][l], 8),
                               (a["conv_w"][l].rearrange("t c -> (t c)"), 32), (a["hg_norm"][l], 4),
                               (a["ssd_norm"][l], 4), (a["lb_param"][l], 4)):
                    pool.dma_start(vin[r:r + k, l], src.rearrange("(k p) -> k p", p=P)).then_inc(S("vec_in"), 16)
                    r += k
                pool.dma_start(wdt[:, l], a["w_in"][l, :, NIN - NH:NIN].rearrange("(k p) n -> p k n", p=P)
                               ).then_inc(S("small_in"), 16)
                pool.dma_start(bc[:, l, 0], a["dt_bias"][l].partition_broadcast(P)).then_inc(S("small_in"), 16)
                pool.dma_start(bc[:, l, 1], a["a_log"][l].partition_broadcast(P)).then_inc(S("small_in"), 16)
                pool.dma_start(bc[:, l, 2], a["d_skip"][l].partition_broadcast(P)).then_inc(S("small_in"), 16)
            pool.dma_start(wro[:], a["w_router"][0].rearrange("(k p) n -> p k n", p=P)).then_inc(S("small_in"), 16)

            for l in range(DEPTH):
                if l == 0:
                    pool.wait_ge(S("tab_round"), 1)
                else:
                    pool.wait_ge(S("used"), PLAN["in", l])
                pool.dma_start(cst[:], a["state_conv"][l].rearrange("b r c -> (b r) c")).then_inc(S("cst_in"), 16)
                nc.gpsimd.memset(xbc[:, :, 0:3], 0.0).then_inc(S("pad_zero"), 1)
                pool.wait_ge(S("cso_done"), 2 * l + 2)
                pool.dma_start(conv_p[l, 0], cso[0:3, :]).then_inc(S("conv_stored"), 16)
                pool.dma_start(conv_s[l].rearrange("b r c -> (b r) c"), cso[3:27, :]).then_inc(S("conv_stored"), 16)

                def slab_dram(k, tensors):
                    if k < 8:
                        return tensors[0][l, k].rearrange("h k v -> k h v")
                    return tensors[1][l, k - 8].rearrange("h n p -> n h p")

                def slab_view(k):
                    return slab[:, k % 4, :].rearrange("p (h v) -> p h v", h=H if k < 8 else NH)

                def slab_load(k):
                    use = l * 4 + k // 4
                    if use:
                        pool.wait_ge(slab_out[k % 4], 16 * use)
                    pool.dma_start(slab_view(k), slab_dram(k, (a["state_hgrn"], a["state_ssm"]))
                                   ).then_inc(slab_in[k % 4], 16)

                def slab_store(k):
                    pool.wait_ge(S("slab_done"), l * 16 + k + 1)
                    pool.dma_start(slab_dram(k, (hg_s, ssm_s)), slab_view(k)).then_inc(slab_out[k % 4], 16)

                for k in range(4):
                    slab_load(k)
                pool.wait_ge(S("sh_done"), 2 * l + 2)
                pool.dma_start(hg_p[l, 0].rearrange("h k v -> k h v"),
                               SH[:].rearrange("p (h v) -> p h v", h=H)).then_inc(S("hgp_stored"), 16)
                pool.wait_ge(S("conv_stored"), 32 * (l + 1))
                for b in range(NSQ):
                    if b == 0:
                        pool.wait_ge(S("kd_done"), LT(l, 2) + 1)
                    if b >= 2:
                        pool.wait_ge(S("sst_mm"), l * 8 + b - 1)
                    nc.gpsimd.tensor_scalar(kdm[:, b % 2], kd[0:NS], tabv("seq")[0:NS, b:b + 1], None, ALU.mult
                                            ).then_inc(S("kdm_done"), 1)
                    if b >= 1:
                        slab_store(b - 1)
                        slab_load(b + 3)
                slab_store(7)
                slab_load(11)
                for b in range(NSQ):
                    if b == 0:
                        pool.wait_ge(S("Bt_done"), LT(l, 2) + 1)
                        pool.wait_ge(S("kdm_done"), l * 8 + 8)
                    if b >= 2:
                        pool.wait_ge(S("bst_mm"), l * 8 + b - 1)
                    nc.gpsimd.tensor_scalar(Bm[:, b % 2], Bt[0:NS], tabv("seq")[0:NS, b:b + 1], None, ALU.mult
                                            ).then_inc(S("Bm_done"), 1)
                    if b >= 1:
                        slab_store(8 + b - 1)
                        if b + 3 < 8:
                            slab_load(8 + b + 3)
                slab_store(15)
                pool.wait_ge(S("ss_done"), 2 * l + 2)
                pool.dma_start(ssm_p[l, 0].rearrange("h n p -> n h p"),
                               SS[:].rearrange("p (h v) -> p h v", h=NH)).then_inc(S("ssp_stored"), 16)
                for k in range(4):
                    pool.wait_ge(slab_out[k], 16 * 4 * (l + 1))
                pool.wait_ge(S("hgp_stored"), 16 * (l + 1))
                pool.wait_ge(S("ssp_stored"), 16 * (l + 1))
                pool.sem_inc(S("mixer_stored"), 1)

            pool.wait_ge(S("moe_sum"), 1)
            pool.dma_start(gfin[:], a["norm_final"].partition_broadcast(P)).then_inc(S("gfin_in"), 16)
            for t, (o, n) in enumerate(TILES):
                pool.wait_ge(S("y_done"), t + 1)
                dst = y_prompt[0, o:o + n] if t < 2 else y_sample.rearrange("b s d -> (b s) d")
                pool.dma_start(dst, ht[0:n, t]).then_inc(S("y_out"), 16)
            pool.wait_ge(S("y_out"), 48)

        @block.scalar
        def _(act):
            A = nc.scalar.activation
            steps = [0]

            def own(ins):
                steps[0] += 1
                ins.then_inc(S("act_step"), 1)
                act.wait_ge(S("act_step"), steps[0])

            def split_hi(u, n=UN):
                if u >= PLAN["down", 0] and u < PLAN["in", 1]:
                    n = 1408
                act.wait_ge(landed[u % RING], 16 * (u // RING + 1))
                if u >= 2:
                    act.wait_ge(S("used"), u - 1)
                A(spH[:, u % 2, 0:n], raw(u, n), ACT.Copy).then_inc(S("hi_done"), 1)

            def norm_t(k, src_ready, val, sqv):
                act.wait_ge(src_ready, val)
                A(sqv[:], xT[:], ACT.Square).then_inc(S("sq_done"), 1)
                act.wait_ge(S("ss_mm"), k + 1)
                if k == 0:
                    act.wait_ge(S("eps_set"), 1)
                own(A(rstd[:], ps[:, 0, 0:TOK], ACT.Ln, bias=eps[:, 0:1], scale=1.0 / D))
                A(rstd[:], rstd[:], ACT.Exp, scale=-0.5).then_inc(S("rstd_done"), 1)
                act.wait_ge(S("hn_f"), k + 1)
                A(hnH[:], sqv[:], ACT.Copy).then_inc(S("hnH_done"), 1)

            act.wait_ge(S("stage_in"), 16)
            A(tabR[:], stage[:], ACT.Copy).then_inc(S("tab_round"), 1)
            for t, (o, n) in enumerate(TILES):
                for half in range(2):
                    i = 2 * t + half
                    act.wait_ge(S("xin_tr"), i + 1)
                    A(xT[:, 4 * half:4 * half + 4, o:o + n],
                      ps[:, 2 + i % 2, 0:4 * n].rearrange("p (k n) -> p k n", k=4), ACT.Copy
                      ).then_inc(S("xT_done"), 1)
            act.wait_ge(S("small_in"), 16 * (4 * DEPTH + 1))
            A(bc[:, :, 1], bc[:, :, 1], ACT.Exp).then_inc(S("aexp_done"), 1)
            act.wait_ge(S("lb_max"), 1)
            A(lbt[:, 0:2], lbt[:, 0:2], ACT.Exp).then_inc(S("lb_exp"), 1)

            for l in range(DEPTH):
                u = PLAN["in", l]
                split_hi(u)
                split_hi(u + 1)
                if l == 0:
                    norm_t(0, S("xT_done"), 6, sq)
                else:
                    norm_t(2, S("down_evac"), 8, sq)
                act.wait_ge(S("cst_tr"), l + 1)
                for k in range(8):
                    dst = xbc[:, k, 3 + NPR:PADC].rearrange("p (b r) -> p b r", b=NSQ)[:, :, 0:3]
                    A(dst, ps[:, 6, 24 * k:24 * k + 24].rearrange("p (b r) -> p b r", b=NSQ), ACT.Copy
                      ).then_inc(S("pads_done"), 1)
                for c in range(7):
                    split_hi(u + 2 * c + 2)
                    split_hi(u + 2 * c + 3)
                    if c == C_F:
                        continue
                    act.wait_ge(S("used"), u + 2 * c + 2)
                    bank = 4 * (c % 2)
                    src = ps[:, bank:bank + 4, 0:TOK]
                    if c in (C_XS, C_BC):
                        m = 4 * c
                        A(xbc[:, m:m + 4, 3:3 + NPR], src[:, :, 0:NPR], ACT.Copy)
                        for k in range(4):
                            dst = xbc[:, m + k, 3 + NPR:PADC].rearrange("p (b r) -> p b r", b=NSQ)[:, :, 3:]
                            ins = A(dst, src[:, k, NPR:TOK].rearrange("p (b r) -> p b r", b=NSQ), ACT.Copy)
                        ins.then_inc(S("proj_evac"), 1)
                    elif c in (C_Q, C_OG, C_Z):
                        A({C_Q: qT, C_OG: ogT, C_Z: zT}[c][:], src, ACT.Silu).then_inc(S("proj_evac"), 1)
                    else:
                        A(oT[:], src, ACT.Copy).then_inc(S("proj_evac"), 1)
                    if c in (C_XS, C_BC):
                        for k in range(4 * c, 4 * c + 4):
                            act.wait_ge(S("conv_sum"), 8 * l + k + 1)
                            A(cvT[:, k, 0:NPR], cvt[:, k % 2, 0:NPR], ACT.Silu)
                            A(cvT[:, k, NPR:TOK].rearrange("p (b r) -> p b r", b=NSQ),
                              cvt[:, k % 2, 3 + NPR:PADC].rearrange("p (b r) -> p b r", b=NSQ)[:, :, 0:LSQ],
                              ACT.Silu).then_inc(S("conv_done"), 1)
                act.wait_ge(S("fz_done"), l + 1)
                own(A(kT[:], lfT[:], ACT.Exp, scale=-1.0))
                own(A(lfT[:], kT[:], ACT.Ln, bias=1.0))
                A(lfT[:], lfT[:], ACT.Exp, scale=-1.0).then_inc(S("sigm_done"), 1)
                act.wait_ge(S("dt_abs"), l + 1)
                own(A(dtb[:, 2], dtb[:, 1], ACT.Exp, scale=-1.0))
                A(dtb[:, 2], dtb[:, 2], ACT.Ln, bias=1.0).then_inc(S("dt_ln"), 1)
                act.wait_ge(S("k_done"), l + 1)
                act.wait_ge(S("lb_done"), 1)
                for h in range(H):
                    A(lfT[:, h], lfT[:, h], ACT.Ln, bias=lbom[:, l, 0, h:h + 1],
                      scale=lbom[:, l, 1, h:h + 1]).then_inc(S("lf_done"), 1)
                for half in range(2):
                    act.wait_ge(S("cso_tr"), 2 * l + half + 1)
                    A(cso[:, 512 * half:512 * half + 512], ps[0:27, 2 + half, :], ACT.Copy
                      ).then_inc(S("cso_done"), 1)

                for t, (o, n) in enumerate(TILES):
                    i = LT(l, t)
                    act.wait_ge(S("lf_tr"), i + 1)
                    A(lfH[0:n], ps[0:n, 4, :], ACT.Copy).then_inc(S("lfH_done"), 1)
                    act.wait_ge(S("kx_mm"), i + 1)
                    A(kd[0:n], ps[0:n, 7, :], ACT.Exp).then_inc(S("kx_exp"), 1)
                    act.wait_ge(S("v_tr"), i + 1)
                    A(vtk[0:n], ps[0:n, 4, :], ACT.Copy).then_inc(S("v_done"), 1)
                    for h in range(H):
                        j = LTH(l, t, h)
                        act.wait_ge(S("x_mm"), j + 1)
                        if j:
                            act.wait_ge(S("y_done2"), j)
                        if t < 2:
                            A(M[:].rearrange("p v n -> p (v n)"), ps[:, 0:2, :].rearrange("p b n -> p (b n)"),
                              ACT.Exp).then_inc(S("x_exp"), 1)
                        else:
                            A(M[:].rearrange("p v n -> p (v n)")[:, 0:(LS + 1) * n], ps[:, 0, 0:(LS + 1) * n],
                              ACT.Exp).then_inc(S("x_exp"), 1)
                    act.wait_ge(S("o_mm"), H * (i + 1))
                    A(oT[:, :, o:o + n], ps[:, 6, 0:H * n].rearrange("p (h n) -> p h n", h=H), ACT.Copy
                      ).then_inc(S("o_evac"), 1)

                for t, (o, n) in enumerate(TILES):
                    i = LT(l, t)
                    act.wait_ge(S("w_mm"), i + 1)
                    if t:
                        act.wait_ge(S("xw_done"), i)
                        act.wait_ge(S("ss_done"), 2 * l + t)
                    A(wsm[0:n], ps[0:n, 5, 256:264], ACT.Exp).then_inc(S("w_exp"), 1)
                    ne = NH if t < 2 else NSQ * NH
                    A(ea[:, 0:ne], ps[:, 5, 264:264 + ne], ACT.Exp).then_inc(S("ea_exp"), 1)
                    A(Bt[0:n], ps[0:n, 5, 0:256], ACT.Copy).then_inc(S("Bt_done"), 1)
                    act.wait_ge(S("diff_mm"), i + 1)
                    if t == 0:
                        act.wait_ge(S("y_done2"), LTH(l, 2, 3) + 1)
                    else:
                        act.wait_ge(S("yi_mm"), i)
                    for g in range(2):
                        A(M[0:n, 4 * g:4 * g + 4, 0:n], ps[0:n, g, 0:4 * n].rearrange("p (r n) -> p r n", r=4),
                          ACT.Exp).then_inc(S("dec_exp"), 1)
                    act.wait_ge(S("E_mm"), i + 1)
                    if t:
                        act.wait_ge(S("ssd_y"), i)
                    A(EE[:, :, 0:n], ps[:, 2, 0:4 * n].rearrange("p (j n) -> p j n", j=4), ACT.Exp
                      ).then_inc(S("E_exp"), 1)

                act.wait_ge(S("hg_o"), l + 1)
                A(sqh[:], oT[:], ACT.Square).then_inc(S("gsq_done"), 1)
                act.wait_ge(S("z_done"), l + 1)
                A(sqs[:], cvT[:, 0:4], ACT.Square).then_inc(S("gsq_done"), 1)
                act.wait_ge(S("gss_mm"), l + 1)
                A(rsh[:], ps[:, 0:4, 0:TOK], ACT.Ln, bias=eps[:, 0:1], scale=1.0 / P)
                own(A(rss[:], ps[:, 4:6, 0:TOK], ACT.Ln, bias=eps[:, 0:1], scale=0.5 / P))
                A(rsh[:], rsh[:], ACT.Exp, scale=-0.5).then_inc(S("grs_done"), 1)
                A(rss[:], rss[:], ACT.Exp, scale=-0.5).then_inc(S("grs_done"), 1)
                act.wait_ge(S("mixed_f"), 2 * l + 1)
                A(hnH[:, 0:4], oT[:], ACT.Copy).then_inc(S("mixH_done"), 1)
                act.wait_ge(S("mixed_f"), 2 * l + 2)
                A(hnH[:, 4:8], cvT[:, 0:4], ACT.Copy).then_inc(S("mixH_done"), 1)
                uo = PLAN["out", l]
                for k in (2, 3):
                    split_hi(uo + k)
                if l == 0:
                    split_hi(uo + 4)
                    split_hi(uo + 5)
                    act.wait_ge(S("mixer_stored"), 1)
                    norm_t(1, S("out_evac"), 2, sq)
                    uu, ud = PLAN["up", 0], PLAN["down", 0]
                    for j in range(11):
                        split_hi(uu + 2 * j + 2)
                        split_hi(uu + 2 * j + 3)
                        act.wait_ge(S("used"), uu + 2 * j + 2)
                        if j:
                            act.wait_ge(S("hf_done"), j)
                        bank = 4 * (j % 2)
                        A(gs[:], ps[:, bank:bank + 2, 0:TOK], ACT.Silu).then_inc(S("gs_done"), 1)
                        act.wait_ge(S("hf_done"), j + 1)
                        A(hfH[:, 2 * j:2 * j + 2], hf[:], ACT.Copy).then_inc(S("hfH_done"), 1)
                    for m in range(7):
                        split_hi(ud + 2 * m + 2)
                        split_hi(ud + 2 * m + 3)

            act.wait_ge(S("mixer_stored"), 2)
            norm_t(3, S("out_evac"), 4, sqm)
            for t, (o, n) in enumerate(TILES):
                for q in range(4):
                    k = 4 * t + q
                    act.wait_ge(S("tk_tr"), k + 1)
                    dst = hkH if q < 2 else ht
                    A(dst[0:n, t, 512 * (q % 2):512 * (q % 2) + 512], ps[0:n, 4 + k % 2, :], ACT.Copy
                      ).then_inc(S("tk_done"), 1)
            act.wait_ge(S("rt_diff"), 1)
            A(sml[:, 9, :, 0:1], sml[:, 8, :, 0:1], ACT.Exp).then_inc(S("rt_exp"), 1)

            def expert_hi(it, j):
                src, sem, before = eslot(j)
                act.wait_ge(sem, it * (16 * EU // ERING) + 16 * (before + j // ERING + 1))
                act.wait_ge(S("used"), it * EU + (U0 + j - AHEAD + 1))
                A(esplit(j)[0], src, ACT.Copy).then_inc(S("hi_done"), 1)

            def gathered(it):
                for q in range(4):
                    act.wait_ge(S("gath_mm"), it * 4 + (q + 1))
                    A((XH if q < 2 else XL)[:, 4 * (q % 2):4 * (q % 2) + 4],
                      ps[:, 2 + q % 2, :].rearrange("p (k n) -> p k n", k=4), ACT.Copy).then_inc(S("X_done"), 1)

            def expert_act(it):
                for p in range(EU):
                    if p in UP_LAST:
                        c = UP_LAST.index(p)
                        act.wait_ge(S("used"), it * EU + (U0 + p + 1))
                        act.wait_ge(S("eh_done"), it * EC + (c + 1))
                        A(sg[:, 0], ps[:, 2 * (c % 2), :], ACT.Silu).then_inc(S("sg_done"), 1)
                    if p in TURN_AT:
                        c = TURN_AT.index(p)
                        act.wait_ge(S("eh_tr"), it * EC + (c + 1))
                        A(hTH[:], ps[:, 4, :].rearrange("p (k n) -> p k n", k=4), ACT.Copy
                          ).then_inc(S("hTH_done"), 1)
                    expert_hi(it, p + AHEAD)
                    if p == UP_LAST[-1]:
                        gathered(it + 1)
                act.wait_ge(S("used"), it * EU + (U0 + EU))
                for q in range(2):
                    A(yH[:, 512 * q:512 * q + 512], ps[:, 6 + q, :], ACT.Copy).then_inc(S("yH_done"), 1)

            for j in range(AHEAD):
                expert_hi(0, j)
            gathered(0)
            with act.Fori(0, NE) as e:
                expert_act(e)
            act.wait_ge(S("rounds_ready"), 1)
            rounds = act.value_load(rndi[0:1, 0:1], min_val=1, max_val=MAXR)
            with act.If(rounds > 1):
                with act.Fori(1, rounds) as r:
                    with act.Fori(0, NE) as e:
                        expert_act(act.snap(r * NE + e))
            act.wait_ge(S("moe_sum"), 1)
            for t, (o, n) in enumerate(TILES):
                A(fsq[0:n, t], ht[0:n, t], ACT.Square).then_inc(S("fsq_done"), 1)
            act.wait_ge(S("fss_sum"), 3)
            for t, (o, n) in enumerate(TILES):
                own(A(fss[0:n, t:t + 1], fss[0:n, t:t + 1], ACT.Ln, bias=eps[0:n, 0:1], scale=1.0 / D))
            for t, (o, n) in enumerate(TILES):
                A(fss[0:n, t:t + 1], fss[0:n, t:t + 1], ACT.Exp, scale=-0.5).then_inc(S("frs_done"), 1)

        @block.vector
        def _(dve):
            V = nc.vector
            steps = [0]

            def own(ins):
                steps[0] += 1
                ins.then_inc(S("dve_step"), 1)
                dve.wait_ge(S("dve_step"), steps[0])

            def split_lo(u):
                n = 1408 if PLAN["down", 0] <= u < PLAN["in", 1] else UN
                dve.wait_ge(S("hi_done"), u + 1)
                V.tensor_tensor(spL[:, u % 2, 0:n], raw(u, n), spH[:, u % 2, 0:n].bitcast(F32), ALU.subtract
                                ).then_inc(S("split_done"), 1)

            def norm_t(k, l, which, sqv):
                dve.wait_ge(S("rstd_done"), k + 1)
                for i in range(KT):
                    ins = V.scalar_tensor_tensor(out=sqv[:, i], in0=xT[:, i],
                                                 scalar=vec[:, l, which * 8 + i:which * 8 + i + 1],
                                                 in1=rstd[:], op0=ALU.mult, op1=ALU.mult)
                ins.then_inc(S("hn_f"), 1)
                dve.wait_ge(S("hnH_done"), k + 1)
                V.tensor_tensor(hnL[:], sqv[:], hnH[:].bitcast(F32), ALU.subtract).then_inc(S("hnL_done"), 1)

            dve.wait_ge(S("vec_tr"), 1)
            own(V.tensor_copy(vec[:], ps[:, 1, 0:DEPTH * 68].rearrange("p (l n) -> p l n", l=DEPTH)))
            own(V.tensor_tensor(lbt[:, 2], vec[:, 0, 64:68], vec[:, 1, 64:68], ALU.max))
            own(V.tensor_tensor(lbt[:, 0], vec[:, 0, 64:68], lbt[:, 2], ALU.subtract))
            V.tensor_tensor(lbt[:, 1], vec[:, 1, 64:68], lbt[:, 2], ALU.subtract).then_inc(S("lb_max"), 1)
            own(V.memset(lbom[:, 0, 0], 0.0))
            own(V.memset(lbom[:, 0, 1], 1.0))
            own(V.memset(dtb[:], 0.0))
            dve.wait_ge(S("lb_exp"), 1)
            own(V.tensor_tensor(lbt[:, 2], lbt[:, 0], lbt[:, 1], ALU.add))
            own(V.reciprocal(lbt[:, 3], lbt[:, 2]))
            own(V.tensor_tensor(lbom[:, 1, 0], lbt[:, 1], lbt[:, 3], ALU.mult))
            V.tensor_tensor(lbom[:, 1, 1], lbt[:, 0], lbt[:, 3], ALU.mult).then_inc(S("lb_done"), 1)

            for l in range(DEPTH):
                u = PLAN["in", l]
                split_lo(u)
                split_lo(u + 1)
                norm_t(2 * l, l, 0, sq)
                dve.wait_ge(S("dt_mm"), l + 1)
                dve.wait_ge(S("small_in"), 16 * (4 * DEPTH + 1))
                if l:
                    own(V.memset(dtb[:], 0.0))
                own(V.tensor_copy(dtb[:, 0, 0:2], ps[:, 7, 0:16].rearrange("p (t n) -> p t n", t=2)))
                V.tensor_copy(dtb[0:NS, 0, 2], ps[0:NS, 7, 16:24]).then_inc(S("dt_evac"), 1)
                dve.wait_ge(S("dt_evac"), l + 1)
                own(V.tensor_tensor(dtb[:, 0], dtb[:, 0], bc[:, l, 0].unsqueeze(1).broadcast_to([P, 3, NH]), ALU.add))
                V.scalar_tensor_tensor(out=dtb[:, 1], in0=dtb[:, 0], scalar=-1.0, in1=dtb[:, 0],
                                       op0=ALU.mult, op1=ALU.max).then_inc(S("dt_abs"), 1)
                for c in range(7):
                    split_lo(u + 2 * c + 2)
                    split_lo(u + 2 * c + 3)
                    if c == C_F:
                        dve.wait_ge(S("used"), u + 2 * c + 2)
                        V.tensor_scalar(lfT[:], ps[:, 4:8, 0:TOK], -40.0, None, ALU.max).then_inc(S("fz_done"), 1)
                    if c in (C_XS, C_BC):
                        dve.wait_ge(S("proj_evac"), 6 * l + c + 1)
                        dve.wait_ge(S("pad_zero"), l + 1)
                        w = PADC - TAPS + 1
                        for k in range(4 * c, 4 * c + 4):
                            if k >= 2:
                                dve.wait_ge(S("conv_done"), 8 * l + k - 1)
                            own(V.tensor_scalar(cvt[:, k % 2, 0:w], xbc[:, k, 0:w], vec[:, l, 24 + k:25 + k],
                                                vec[:, l, 16 + k:17 + k], ALU.mult, ALU.add))
                            for tap in range(1, TAPS):
                                i = V.scalar_tensor_tensor(
                                    out=cvt[:, k % 2, 0:w], in0=xbc[:, k, tap:tap + w],
                                    scalar=vec[:, l, 24 + 8 * tap + k:25 + 8 * tap + k],
                                    in1=cvt[:, k % 2, 0:w], op0=ALU.mult, op1=ALU.add)
                                if tap < TAPS - 1:
                                    own(i)
                                else:
                                    i.then_inc(S("conv_sum"), 1)
                        if c == C_BC:
                            dve.wait_ge(S("cst_tr"), l + 1)
                            own(V.tensor_copy(cpk[:, :, 0:3], xbc[:, :, NPR:NPR + 3]))
                            for k in range(8):
                                V.tensor_copy(cpk[:, k, 3:27].rearrange("p (b r) -> p b r", b=NSQ),
                                              xbc[:, k, 3 + NPR:PADC].rearrange("p (b r) -> p b r", b=NSQ)[:, :, 8:11]
                                              ).then_inc(S("cpk_done"), 1)
                dve.wait_ge(S("sigm_done"), l + 1)
                dve.wait_ge(S("lb_done"), 1)
                for h in range(H):
                    ins = V.scalar_tensor_tensor(out=kT[:, h], in0=kT[:, h], scalar=lbom[:, l, 1, h:h + 1],
                                                 in1=lfT[:, h], op0=ALU.mult, op1=ALU.mult)
                ins.then_inc(S("k_done"), 1)
                dve.wait_ge(S("dt_ln"), l + 1)
                dve.wait_ge(S("aexp_done"), 1)
                own(V.scalar_tensor_tensor(out=dtb[:, 3], in0=dtb[:, 0], scalar=0.0, in1=dtb[:, 2],
                                           op0=ALU.max, op1=ALU.add))
                V.scalar_tensor_tensor(out=dtb[:, 4], in0=dtb[:, 3], scalar=-1.0,
                                       in1=bc[:, l, 1].unsqueeze(1).broadcast_to([P, 3, NH]),
                                       op0=ALU.mult, op1=ALU.mult).then_inc(S("a_done"), 1)

                for t, (o, n) in enumerate(TILES):
                    i = LT(l, t)
                    nl = LV if t < 2 else LS
                    flat = lambda x: x[:].rearrange("p v n -> p (v n)")
                    Mv = flat(M)[:, 0:(nl + 1) * n].rearrange("p (v n) -> p v n", n=n)
                    Yqv = flat(Yq)[:, 0:(nl + 1) * n].rearrange("p (v n) -> p v n", n=n)
                    Ykv = flat(Yk)[:, 0:nl * n].rearrange("p (v n) -> p v n", n=n)
                    SCv = flat(SC)[:, 0:(nl + 1) * n]
                    dve.wait_ge(S("lfH_done"), i + 1)
                    V.tensor_tensor(lfL[0:n], ps[0:n, 4, :], lfH[0:n].bitcast(F32), ALU.subtract
                                    ).then_inc(S("lfL_done"), 1)
                    dve.wait_ge(S("kx_exp"), i + 1)
                    dve.wait_ge(S("k_tr"), i + 1)
                    V.tensor_tensor(kd[0:n], kd[0:n], ps[0:n, 5, :], ALU.mult).then_inc(S("kd_done"), 1)
                    for h in range(H):
                        j = LTH(l, t, h)
                        dve.wait_ge(S("x_exp"), j + 1)
                        if j:
                            dve.wait_ge(S("o_mm"), j)
                        q_b = qT[:, h, o:o + n].unsqueeze(1).broadcast_to([P, nl + 1, n])
                        k_b = kT[:, h, o:o + n].unsqueeze(1).broadcast_to([P, nl, n])
                        V.tensor_tensor(Yqv, Mv, q_b, ALU.mult)
                        if t < 2:
                            own(V.tensor_copy(egl[:, h, 0:1], Mv[:, nl, n - 1:n]))
                        else:
                            own(V.tensor_copy(egl[:, h], Mv[:, nl, LSQ - 1:n:LSQ]))
                            V.tensor_tensor(qG[:, h], Mv[:, nl], qT[:, h, o:o + n], ALU.mult
                                            ).then_inc(S("qG_done"), 1)
                        V.tensor_tensor(Ykv, Mv[:, 0:nl], k_b, ALU.mult).then_inc(S("y_done2"), 1)
                        dve.wait_ge(S("sc_mm"), j + 1)
                        if t < 2:
                            V.tensor_tensor(SCv, ps[:, 2:4, :].rearrange("p b n -> p (b n)"), tabv("mask"), ALU.mult
                                            ).then_inc(S("sc_done"), 1)
                        else:
                            V.tensor_tensor(SCv[0:n], ps[0:n, 2, 0:(nl + 1) * n], tabv("ms")[0:n], ALU.mult
                                            ).then_inc(S("sc_done"), 1)
                    if t < 2:
                        dve.wait_ge(S("st_mm"), 2 * l + t + 1)
                        if t == 0:
                            if l:
                                dve.wait_ge(S("hgp_stored"), 16 * l)
                            V.tensor_copy(SH[:], ps[:, 7, :]).then_inc(S("sh_done"), 1)
                        else:
                            for h in range(H):
                                c0 = h * P
                                ins = V.scalar_tensor_tensor(out=SH[:, c0:c0 + P], in0=SH[:, c0:c0 + P],
                                                       scalar=egl[:, h, 0:1], in1=ps[:, 7, c0:c0 + P],
                                                       op0=ALU.mult, op1=ALU.add)
                            ins.then_inc(S("sh_done"), 1)
                for b in range(NSQ):
                    dve.wait_ge(S("sst_mm"), l * 8 + b + 1)
                    sv = slab[:, b % 4, :].rearrange("p (h v) -> p h v", h=H)
                    own(V.tensor_tensor(sv, sv, egl[:, :, b:b + 1].broadcast_to([P, H, P]), ALU.mult))
                    V.tensor_tensor(slab[:, b % 4, :], slab[:, b % 4, :], ps[:, 4 + b % 2, :], ALU.add
                                    ).then_inc(S("slab_done"), 1)
                dve.wait_ge(S("o_evac"), LT(l, 2) + 1)
                V.tensor_tensor(oT[:, :, NPR:TOK], oT[:, :, NPR:TOK],
                                ps[:, 3, 0:H * NS].rearrange("p (h n) -> p h n", h=H), ALU.add
                                ).then_inc(S("hg_o"), 1)

                for t, (o, n) in enumerate(TILES):
                    i = LT(l, t)
                    Lt = (tabv("l") if t < 2 else tabv("ls"))[0:n, 0:n]
                    Ut = tabv("w")[:, LV * P:] if t < 2 else tabv("ws")[0:n, LS * n:]
                    av = dtb[0:n, 4, t]
                    if t == 0:
                        dve.wait_ge(S("o_mm"), LTH(l, 2, 3) + 1)
                        dve.wait_ge(S("sst_mm"), l * 8 + 8)
                        dve.wait_ge(S("conv_stored"), 32 * (l + 1))
                    else:
                        dve.wait_ge(S("E_mm"), i)
                        dve.wait_ge(S("yi_mm"), i)
                    V.tensor_tensor(La[0:n, :, 0:n], Lt.unsqueeze(1).broadcast_to([n, NH, n]),
                                    av.unsqueeze(2).broadcast_to([n, NH, n]), ALU.mult).then_inc(S("La_done"), 1)
                    V.tensor_copy(aex[0:n], av.unsqueeze(2).broadcast_to([n, NH, HD])).then_inc(S("aex_done"), 1)
                    if t == 2:
                        V.tensor_tensor(am[0:n], av.unsqueeze(1).broadcast_to([n, NSQ, NH]),
                                        tabv("seq")[0:n].unsqueeze(2).broadcast_to([n, NSQ, NH]), ALU.mult
                                        ).then_inc(S("am_done"), 1)
                    dve.wait_ge(S("xs_tr"), i + 1)
                    if t:
                        dve.wait_ge(S("yi_mm"), i)
                    xv = xdt[0:n].rearrange("p (h d) -> p h d", h=NH)
                    own(V.tensor_tensor(xv, ps[0:n, 4, :].rearrange("p (h d) -> p h d", h=NH),
                                        dtb[0:n, 3, t].unsqueeze(2).broadcast_to([n, NH, HD]), ALU.mult))
                    dve.wait_ge(S("w_exp"), i + 1)
                    V.tensor_tensor(xw[0:n].rearrange("p (h d) -> p h d", h=NH), xv,
                                    wsm[0:n].unsqueeze(2).broadcast_to([n, NH, HD]), ALU.mult
                                    ).then_inc(S("xw_done"), 1)
                    dve.wait_ge(S("cb_mm"), i + 1)
                    own(V.tensor_tensor(CBm[0:n, :, 0:n], ps[0:n, 3, 0:2 * n].rearrange("p (g n) -> p g n", g=G),
                                        Ut.unsqueeze(1).broadcast_to([n, G, n]), ALU.mult))
                    for g in range(G):
                        dve.wait_ge(S("dec_exp"), 2 * i + g + 1)
                        V.tensor_tensor(M[0:n, 4 * g:4 * g + 4, 0:n], M[0:n, 4 * g:4 * g + 4, 0:n],
                                        CBm[0:n, g, 0:n].unsqueeze(1).broadcast_to([n, 4, n]), ALU.mult
                                        ).then_inc(S("P_done"), 1)
                    if t == 2:
                        dve.wait_ge(S("ea_exp"), i + 1)
                        eav = ea[:].rearrange("p (b h) -> p b h", b=NSQ)
                        for b in range(NSQ):
                            dve.wait_ge(S("bst_mm"), l * 8 + b + 1)
                            sv = slab[:, b % 4, :].rearrange("p (h v) -> p h v", h=NH)
                            own(V.tensor_tensor(sv, sv, eav[:, b].unsqueeze(2).broadcast_to([P, NH, HD]), ALU.mult))
                            V.tensor_tensor(slab[:, b % 4, :], slab[:, b % 4, :], ps[:, 4 + b % 2, :], ALU.add
                                            ).then_inc(S("slab_done"), 1)
                    if t:
                        dve.wait_ge(S("E_exp"), i + 1)
                        dve.wait_ge(S("yx_mm"), (2 * l + t) if t == 1 else (2 * l + 2))
                        own(V.tensor_tensor(t1[:, :, 0:n], EE[:, :, 0:n],
                                            ps[:, 2, 0:4 * n].rearrange("p (j n) -> p j n", j=4), ALU.mult))
                    dve.wait_ge(S("yi_mm"), i + 1)
                    for j in range(4):
                        for hh in range(2):
                            q0, q1 = hh * HD, (hh + 1) * HD
                            ins = V.scalar_tensor_tensor(
                                out=cvT[q0:q1, j, o:o + n], in0=cvT[q0:q1, j, o:o + n],
                                scalar=bc[q0:q1, l, 2, 2 * j + hh:2 * j + hh + 1],
                                in1=ps[q0:q1, 6, j * n:(j + 1) * n], op0=ALU.mult, op1=ALU.add)
                    if t == 0:
                        ins.then_inc(S("ssd_y"), 1)
                    else:
                        own(ins)
                        V.tensor_tensor(cvT[:, 0:4, o:o + n], cvT[:, 0:4, o:o + n], t1[:, :, 0:n], ALU.add
                                        ).then_inc(S("ssd_y"), 1)
                    if t < 2:
                        dve.wait_ge(S("hst_mm"), 2 * l + t + 1)
                        dve.wait_ge(S("ea_exp"), i + 1)
                        if t == 0:
                            if l:
                                dve.wait_ge(S("ssp_stored"), 16 * l)
                            V.tensor_copy(SS[:], ps[:, 7, :]).then_inc(S("ss_done"), 1)
                        else:
                            sv = SS[:].rearrange("p (h v) -> p h v", h=NH)
                            own(V.tensor_tensor(sv, sv, ea[:, 0:NH].unsqueeze(2).broadcast_to([P, NH, HD]), ALU.mult))
                            V.tensor_tensor(SS[:], SS[:], ps[:, 7, :], ALU.add).then_inc(S("ss_done"), 1)
                dve.wait_ge(S("ssd_y"), 3 * l + 3)
                V.tensor_tensor(cvT[:, 0:4], cvT[:, 0:4], zT[:], ALU.mult).then_inc(S("z_done"), 1)
                dve.wait_ge(S("gsq_done"), 2 * l + 1)
                own(V.tensor_tensor(oT[:], oT[:], ogT[:], ALU.mult))
                dve.wait_ge(S("grs_done"), 2 * l + 1)
                for h in range(H):
                    ins = V.scalar_tensor_tensor(out=oT[:, h], in0=oT[:, h], scalar=vec[:, l, 56 + h:57 + h],
                                                 in1=rsh[:, h], op0=ALU.mult, op1=ALU.mult)
                ins.then_inc(S("mixed_f"), 1)
                dve.wait_ge(S("grs_done"), 2 * l + 2)
                for j in range(4):
                    ins = V.scalar_tensor_tensor(out=cvT[:, j], in0=cvT[:, j], scalar=vec[:, l, 60 + j:61 + j],
                                                 in1=rss[:, j // 2], op0=ALU.mult, op1=ALU.mult)
                ins.then_inc(S("mixed_f"), 1)
                dve.wait_ge(S("mixH_done"), 2 * l + 1)
                V.tensor_tensor(hnL[:, 0:4], oT[:], hnH[:, 0:4].bitcast(F32), ALU.subtract).then_inc(S("mixL_done"), 1)
                dve.wait_ge(S("mixH_done"), 2 * l + 2)
                V.tensor_tensor(hnL[:, 4:8], cvT[:, 0:4], hnH[:, 4:8].bitcast(F32), ALU.subtract
                                ).then_inc(S("mixL_done"), 1)
                uo = PLAN["out", l]
                for c in range(2):
                    if c == 0 or l == 0:
                        split_lo(uo + 2 * c + 2)
                        split_lo(uo + 2 * c + 3)
                    dve.wait_ge(S("used"), uo + 2 * c + 2)
                    V.tensor_tensor(xT[:, 4 * c:4 * c + 4], xT[:, 4 * c:4 * c + 4], ps[:, 4 * c:4 * c + 4, 0:TOK],
                                    ALU.add).then_inc(S("out_evac"), 1)
                if l == 0:
                    norm_t(1, 0, 1, sq)
                    uu, ud = PLAN["up", 0], PLAN["down", 0]
                    for j in range(11):
                        split_lo(uu + 2 * j + 2)
                        split_lo(uu + 2 * j + 3)
                        bank = 4 * (j % 2) + 2
                        dve.wait_ge(S("gs_done"), j + 1)
                        if j:
                            dve.wait_ge(S("hfH_done"), j)
                            dve.wait_ge(S("hfL_done"), j)
                        V.tensor_tensor(hf[:], gs[:], ps[:, bank:bank + 2, 0:TOK], ALU.mult).then_inc(S("hf_done"), 1)
                        dve.wait_ge(S("hfH_done"), j + 1)
                        V.tensor_tensor(hfL[:, 2 * j:2 * j + 2], hf[:], hfH[:, 2 * j:2 * j + 2].bitcast(F32),
                                        ALU.subtract).then_inc(S("hfL_done"), 1)
                    for m in range(8):
                        if m < 7:
                            split_lo(ud + 2 * m + 2)
                            split_lo(ud + 2 * m + 3)
                        dve.wait_ge(S("used"), ud + 2 * m + 2)
                        V.tensor_tensor(xT[:, m], xT[:, m], ps[:, m, 0:TOK], ALU.add).then_inc(S("down_evac"), 1)

            norm_t(3, 1, 1, sqm)
            T = lambda k: sml[:, k]
            one = lambda v: v[:, :, 0:1].broadcast_to([P, 3, NE])
            dve.wait_ge(S("mixer_stored"), 2)
            own(V.memset(T(0), 0.0))
            dve.wait_ge(S("lg_mm"), 1)
            own(V.tensor_copy(sml[:, 0, 0:2], ps[:, 1, 0:16].rearrange("p (t n) -> p t n", t=2)))
            own(V.tensor_copy(sml[0:NS, 0, 2], ps[0:NS, 1, 16:24]))
            io8 = tabv("iota")[:, 0:NE].unsqueeze(1).broadcast_to([P, 3, NE])

            def choose(src, top, hot):
                own(V.tensor_reduce(sml[:, top, :, 0:1], T(src), AX.X, ALU.max))
                own(V.tensor_tensor(T(hot), T(src), one(T(top)), ALU.is_equal))
                own(V.tensor_scalar(T(hot), T(hot), -100.0, 100.0, ALU.mult, ALU.add))
                own(V.tensor_tensor(T(hot), T(hot), io8, ALU.add))
                own(V.tensor_reduce(sml[:, 10, :, 0:1], T(hot), AX.X, ALU.min))
                own(V.tensor_tensor(T(hot), io8, one(T(10)), ALU.is_equal))

            choose(0, 1, 2)
            own(V.tensor_scalar(T(3), T(2), -1.0, 1.0, ALU.mult, ALU.add))
            own(V.tensor_tensor(T(3), T(3), T(0), ALU.mult))
            own(V.tensor_scalar(T(4), T(2), -3.0e38, None, ALU.mult))
            own(V.tensor_tensor(T(3), T(3), T(4), ALU.add))
            choose(3, 5, 6)
            V.tensor_tensor(sml[:, 8, :, 0:1], sml[:, 5, :, 0:1], sml[:, 1, :, 0:1], ALU.subtract
                            ).then_inc(S("rt_diff"), 1)
            V.tensor_tensor(T(7), T(2), T(6), ALU.add).then_inc(S("routed"), 1)
            for t, (o, n) in enumerate(TILES):
                for q in range(2):
                    k = 4 * t + q
                    dve.wait_ge(S("tk_done"), k + 1)
                    c0 = 512 * q
                    V.tensor_tensor(hkL[0:n, t, c0:c0 + 512], ps[0:n, 4 + k % 2, :], hkH[0:n, t, c0:c0 + 512].bitcast(F32),
                                    ALU.subtract).then_inc(S("hkL_done"), 1)
            dve.wait_ge(S("rt_exp"), 1)
            own(V.tensor_scalar(sml[:, 11, :, 0:1], sml[:, 9, :, 0:1], 1.0, None, ALU.add))
            own(V.reciprocal(sml[:, 8, :, 0:1], sml[:, 11, :, 0:1]))
            own(V.tensor_tensor(sml[:, 9, :, 0:1], sml[:, 9, :, 0:1], sml[:, 8, :, 0:1], ALU.mult))
            own(V.tensor_tensor(T(2), T(2), one(T(8)), ALU.mult))
            own(V.tensor_tensor(T(6), T(6), one(T(9)), ALU.mult))
            own(V.tensor_tensor(gate[:].rearrange("p e t -> p t e"), T(2), T(6), ALU.add))
            dve.wait_ge(S("routed"), 1)
            dve.wait_ge(S("rank_mm"), 1)
            own(V.memset(T(3), 0.0))
            own(V.tensor_scalar(sml[:, 3, 0:2], ps[:, 1, 32:48].rearrange("p (t n) -> p t n", t=2), 1.0, None, ALU.add))
            own(V.tensor_scalar(sml[0:NS, 3, 2], ps[0:NS, 1, 48:56], 1.0, None, ALU.add))
            own(V.tensor_tensor(T(3), T(3), T(7), ALU.mult))
            own(V.tensor_scalar(rank[:, 0:NE].rearrange("p e t -> p t e"), T(3), -1.0, None, ALU.add))
            own(V.tensor_scalar(rank[:, NE], rank[:, 0], -float(CAP), None, ALU.add))
            own(V.tensor_reduce(rnd[:, 0:1], ps[:, 1, 64:72], AX.X, ALU.max))
            own(V.tensor_scalar(rnd[:, 1:2], rnd[:, 0:1], float(CAP), 1.0, ALU.is_gt, ALU.add))
            for k in range(2, MAXR):
                own(V.tensor_scalar(rnd[:, 2:3], rnd[:, 0:1], float(CAP * k), None, ALU.is_gt))
                own(V.tensor_tensor(rnd[:, 1:2], rnd[:, 1:2], rnd[:, 2:3], ALU.add))
            V.tensor_copy(rndi[:], rnd[:, 1:2]).then_inc(S("rounds_ready"), 1)

            own(V.memset(selT[:].bitcast(F32), 0.0))
            dve.sem_inc(S("eh_done"), 1)
            dve.sem_inc(S("ht_add"), 1)

            def expert_lo(it, j):
                dve.wait_ge(S("hi_done"), it * EU + (U0 + j + 1))
                hi, lo = esplit(j)
                V.tensor_tensor(lo, eslot(j)[0], hi.bitcast(F32), ALU.subtract).then_inc(S("split_done"), 1)

            def one_hot(ranks):
                for t in range(3):
                    i = V.tensor_scalar(sel[:, t], tabv("iota"), ranks[:, t:t + 1], None, ALU.is_equal)
                i.then_inc(S("sel_done"), 1)

            def expert_dve(e, it):
                nxt = dve.snap(e + 1)
                for p in range(EU):
                    if p == 4:
                        dve.wait_ge(S("selT_tr"), it + 1)
                        V.tensor_copy(selT[:].rearrange("p t n -> p (t n)")[:, 0:TOK], ps[:, 5, 0:TOK]
                                      ).then_inc(S("selT_done"), 1)
                        V.tensor_copy(rk[:, 0], rank[:, bass.ds(nxt, 1), :].rearrange("p e t -> p (e t)")
                                      ).then_inc(S("rk_done"), 1)
                        dve.wait_ge(S("rk_done"), it * 2 + 1)
                        one_hot(rk[:, 0])
                    if p in UP_LAST:
                        c = UP_LAST.index(p)
                        dve.wait_ge(S("sg_done"), it * EC + (c + 1))
                        if c:
                            dve.wait_ge(S("eh_tr"), it * EC + c)
                        V.tensor_tensor(sg[:, 1], sg[:, 0], ps[:, 2 * (c % 2) + 1, :], ALU.mult
                                        ).then_inc(S("eh_done"), 1)
                    if p in TURN_AT:
                        c = TURN_AT.index(p)
                        dve.wait_ge(S("hTH_done"), it * EC + (c + 1))
                        V.tensor_tensor(hTL[:], ps[:, 4, :].rearrange("p (k n) -> p k n", k=4), hTH[:].bitcast(F32),
                                        ALU.subtract).then_inc(S("hTL_done"), 1)
                    expert_lo(it, p + AHEAD)
                V.tensor_copy(rk[:, 1], gate[:, bass.ds(e, 1), :].rearrange("p e t -> p (e t)")).then_inc(S("rk_done"), 1)
                for q in range(2):
                    dve.wait_ge(S("yH_done"), it * 2 + (q + 1))
                    V.tensor_tensor(yL[:, 512 * q:512 * q + 512], ps[:, 6 + q, :],
                                    yH[:, 512 * q:512 * q + 512].bitcast(F32), ALU.subtract).then_inc(S("yL_done"), 1)
                dve.wait_ge(S("rk_done"), it * 2 + 2)
                for t, (o, n) in enumerate(TILES):
                    for q in range(2):
                        dve.wait_ge(S("scat_mm"), it * 6 + (2 * t + q + 1))
                        V.scalar_tensor_tensor(out=ht[0:n, t, 512 * q:512 * q + 512], in0=ps[0:n, 2 * t + q, :],
                                               scalar=rk[0:n, 1, t:t + 1], in1=ht[0:n, t, 512 * q:512 * q + 512],
                                               op0=ALU.mult, op1=ALU.add).then_inc(S("ht_add"), 1)

            one_hot(rank[:, 0])
            for j in range(AHEAD):
                expert_lo(0, j)
            with dve.Fori(0, NE) as e:
                expert_dve(e, e)
            rounds = dve.value_load(rndi[0:1, 0:1], min_val=1, max_val=MAXR)
            with dve.If(rounds > 1):
                with dve.Fori(1, rounds) as r:
                    V.tensor_scalar(rank[:], rank[:], -float(CAP), None, ALU.add)
                    dve.drain()
                    with dve.Fori(0, NE) as e:
                        expert_dve(e, dve.snap(r * NE + e))
            dve.drain().then_inc(S("moe_sum"), 1)
            for t, (o, n) in enumerate(TILES):
                dve.wait_ge(S("fsq_done"), t + 1)
                V.tensor_reduce(fss[0:n, t:t + 1], fsq[0:n, t], AX.X, ALU.add).then_inc(S("fss_sum"), 1)
            dve.wait_ge(S("gfin_in"), 16)
            for t, (o, n) in enumerate(TILES):
                dve.wait_ge(S("frs_done"), t + 1)
                V.scalar_tensor_tensor(out=ht[0:n, t], in0=ht[0:n, t], scalar=fss[0:n, t:t + 1], in1=gfin[0:n],
                                       op0=ALU.mult, op1=ALU.mult).then_inc(S("y_done"), 1)

        @block.tensor
        def _(pe):
            mm = nc.tensor.matmul

            def three(out, lhs, rhs, start, stop):
                mm(out, lhs[0], rhs[0], start=start, stop=False)
                mm(out, lhs[0], rhs[1], start=False, stop=False)
                return mm(out, lhs[1], rhs[0], start=False, stop=stop)

            def unit(u, k):
                n = 1408 if PLAN["down", 0] <= u < PLAN["in", 1] else UN
                return [x[:, u % 2, 0:n].rearrange("p (k n) -> p k n", k=k) for x in (spH, spL)]

            def norm_mm(k, sqv):
                pe.wait_ge(S("sq_done"), k + 1)
                for i in range(KT):
                    m = mm(ps[:, 0, 0:TOK], onesf, sqv[:, i], start=i == 0, stop=i == KT - 1)
                m.then_inc(S("ss_mm"), 1)

            pe.wait_ge(S("tab_in"), 16)
            pe.wait_ge(S("vec_in"), 16 * 7 * DEPTH)
            for l in range(DEPTH):
                m = nc.tensor.transpose(ps[:, 1, 68 * l:68 * l + 68], vin[:, l], ident[0:68, 0:68])
            m.then_inc(S("vec_tr"), 1)
            pe.wait_ge(S("x_in"), 48)
            for t, (o, n) in enumerate(TILES):
                for half in range(2):
                    i = 2 * t + half
                    if i >= 2:
                        pe.wait_ge(S("xT_done"), i - 1)
                    for k in range(4):
                        m = nc.tensor.transpose(ps[:, 2 + i % 2, k * n:(k + 1) * n],
                                                xin[0:n, t, (4 * half + k) * P:(4 * half + k + 1) * P],
                                                ident[0:n, 0:n])
                    m.then_inc(S("xin_tr"), 1)
            pe.wait_ge(S("tab_round"), 1)

            for l in range(DEPTH):
                norm_mm(2 * l, sq)
                pe.wait_ge(S("cst_in"), 16 * (l + 1))
                for k in range(8):
                    m = nc.tensor.transpose(ps[:, 6, 24 * k:24 * k + 24], cst[:, k * P:(k + 1) * P], ident[0:24, 0:24])
                m.then_inc(S("cst_tr"), 1)
                pe.wait_ge(S("hnL_done"), 2 * l + 1)
                pe.wait_ge(S("small_in"), 16 * (4 * DEPTH + 1))
                for t, (o, n) in enumerate(TILES):
                    for k in range(KT):
                        mm(ps[0:n, 7, 8 * t:8 * t + 8], hnH[:, k, o:o + n].bitcast(F32), wdt[:, l, k],
                           start=k == 0, stop=False)
                        m = mm(ps[0:n, 7, 8 * t:8 * t + 8], hnL[:, k, o:o + n].bitcast(F32), wdt[:, l, k],
                               start=False, stop=k == KT - 1)
                m.then_inc(S("dt_mm"), 1)

                def dense(u, c):
                    for half in range(2):
                        pe.wait_ge(S("split_done"), u + half + 1)
                        wH, wL = unit(u + half, 4)
                        for i in range(4):
                            for k in range(4):
                                kk = 4 * half + k
                                m = three(ps[:, 4 * (c % 2) + i, 0:TOK],
                                          (wH[:, k, i * P:(i + 1) * P], wL[:, k, i * P:(i + 1) * P]),
                                          (hnH[:, kk], hnL[:, kk]), start=kk == 0, stop=kk == KT - 1)
                        if half == 0:
                            m.then_inc(S("used"), 1)
                    return m

                for c in range(7):
                    if c == 0:
                        pe.wait_ge(S("rstd_done"), 2 * l + 1)
                    if c == 1:
                        pe.wait_ge(S("pads_done"), 8 * (l + 1))
                        pe.wait_ge(S("dt_evac"), l + 1)
                    if c >= 2:
                        pe.wait_ge(S("proj_evac"), 6 * l + c - 1)
                    dense(PLAN["in", l] + 2 * c, c).then_inc(S("used"), 1)

                pe.wait_ge(S("cpk_done"), 8 * (l + 1))
                pe.wait_ge(S("proj_evac"), 6 * (l + 1))
                for half in range(2):
                    for k in range(4):
                        m = nc.tensor.transpose(ps[0:27, 2 + half, k * P:(k + 1) * P], cpk[:, 4 * half + k, :], ident)
                    m.then_inc(S("cso_tr"), 1)

                for t, (o, n) in enumerate(TILES):
                    i = LT(l, t)
                    nl = LV if t < 2 else LS
                    pe.wait_ge(S("lf_done"), H * (l + 1))
                    if t:
                        pe.wait_ge(S("v_done"), i)
                    for h in range(H):
                        m = nc.tensor.transpose(ps[0:n, 4, h * P:(h + 1) * P], lfT[:, h, o:o + n], ident)
                    m.then_inc(S("lf_tr"), 1)
                    if t:
                        pe.wait_ge(S("kd_done"), i)
                    for h in range(H):
                        m = nc.tensor.transpose(ps[0:n, 5, h * P:(h + 1) * P], kT[:, h, o:o + n], ident)
                    m.then_inc(S("k_tr"), 1)
                    pe.wait_ge(S("lfL_done"), i + 1)
                    if t:
                        pe.wait_ge(S("sh_done"), 2 * l + t)
                    Lr = tabv("l", F32R) if t < 2 else tabv("ls", F32R)[0:n]
                    mm(ps[:, 7, :], Lr, lfH[0:n], start=True, stop=False)
                    mm(ps[:, 7, :], Lr, lfL[0:n], start=False, stop=True).then_inc(S("kx_mm"), 1)
                    for h in range(H):
                        m = nc.tensor.transpose(ps[0:n, 4, h * P:(h + 1) * P], oT[:, h, o:o + n], ident)
                    m.then_inc(S("v_tr"), 1)

                    def exponents(h):
                        j = LTH(l, t, h)
                        if h or t:
                            pe.wait_ge(S("x_exp"), j)
                        W = tabv("w", F32R) if t < 2 else tabv("ws", F32R)[0:n]
                        for b in range(2 if t < 2 else 1):
                            w = W[:, 512 * b:512 * b + 512] if t < 2 else W
                            out = ps[:, b, 0:w.shape[1]]
                            mm(out, lfH[0:n, h * P:(h + 1) * P], w, start=True, stop=False)
                            m = mm(out, lfL[0:n, h * P:(h + 1) * P], w, start=False, stop=True)
                        m.then_inc(S("x_mm"), 1)

                    exponents(0)
                    flat = lambda x: x[:].rearrange("p v n -> p (v n)")
                    for h in range(H):
                        j = LTH(l, t, h)
                        if h < H - 1:
                            exponents(h + 1)
                        pe.wait_ge(S("y_done2"), j + 1)
                        if j == LTH(l, 0, 0):
                            pe.wait_ge(S("cso_done"), 2 * l + 2)
                        else:
                            pe.wait_ge(S("sc_done"), j)
                        for v in range(nl + 1):
                            out = ps[0:n, 2 + (v * n) // 512, (v * n) % 512:(v * n) % 512 + n]
                            if v < nl:
                                m = mm(out, flat(Yk)[:, v * n:(v + 1) * n], flat(Yq)[:, v * n:(v + 1) * n],
                                       start=True, stop=True)
                            else:
                                m = mm(out, kT[:, h, o:o + n], qT[:, h, o:o + n], start=True, stop=True)
                        m.then_inc(S("sc_mm"), 1)
                        pe.wait_ge(S("sc_done"), j + 1)
                        pe.wait_ge(S("v_done"), i + 1)
                        if h == 0 and t:
                            pe.wait_ge(S("o_evac"), i)
                        out = ps[:, 6, h * n:(h + 1) * n]
                        for v in range(nl + 1):
                            m = mm(out, vtk[0:n, h * P:(h + 1) * P], flat(SC)[0:n, v * n:(v + 1) * n],
                                   start=v == 0, stop=v == nl and t != 1)
                        if t == 1:
                            if h == 0:
                                pe.wait_ge(S("sh_done"), 2 * l + 1)
                            m = mm(out, SH[:, h * P:(h + 1) * P], flat(Yq)[:, nl * n:(nl + 1) * n],
                                   start=False, stop=True)
                        m.then_inc(S("o_mm"), 1)
                    if t < 2:
                        pe.wait_ge(S("kd_done"), i + 1)
                        for h in range(H):
                            m = mm(ps[:, 7, h * P:(h + 1) * P], kd[0:n, h * P:(h + 1) * P],
                                   vtk[0:n, h * P:(h + 1) * P], start=True, stop=True)
                        m.then_inc(S("st_mm"), 1)
                pe.wait_ge(S("qG_done"), H * (l + 1))
                pe.wait_ge(S("kd_done"), LT(l, 2) + 1)
                for b in range(NSQ):
                    pe.wait_ge(slab_in[b % 4], 16 * (4 * l + b // 4 + 1))
                    for h in range(H):
                        mm(ps[:, 3, h * NS + b * LSQ:h * NS + (b + 1) * LSQ], slab[:, b % 4, h * P:(h + 1) * P],
                           qG[:, h, b * LSQ:(b + 1) * LSQ], start=True, stop=True)
                    pe.wait_ge(S("kdm_done"), 8 * l + b + 1)
                    if b >= 2:
                        pe.wait_ge(S("slab_done"), 16 * l + b - 1)
                    for h in range(H):
                        m = mm(ps[:, 4 + b % 2, h * P:(h + 1) * P], kdm[:, b % 2, h * P:(h + 1) * P],
                               vtk[0:NS, h * P:(h + 1) * P], start=True, stop=True)
                    m.then_inc(S("sst_mm"), 1)

                for t, (o, n) in enumerate(TILES):
                    i = LT(l, t)
                    Lf = (tabv("l") if t < 2 else tabv("ls"))[0:n, 0:n]
                    Uf = tabv("w")[:, LV * P:] if t < 2 else tabv("ws")[0:n, LS * n:]
                    if t == 0:
                        pe.wait_ge(S("slab_done"), 16 * l + 8)
                        pe.wait_ge(S("conv_done"), 8 * (l + 1))
                    else:
                        pe.wait_ge(S("xw_done"), i)
                        pe.wait_ge(S("Bt_done"), i)
                    for j in range(4):
                        m = nc.tensor.transpose(ps[0:n, 4, j * P:(j + 1) * P], cvT[:, j, o:o + n], ident)
                    m.then_inc(S("xs_tr"), 1)
                    for g in range(G):
                        m = nc.tensor.transpose(ps[0:n, 5, g * P:(g + 1) * P], cvT[:, 4 + g, o:o + n], ident)
                    pe.wait_ge(S("a_done"), l + 1)
                    mm(ps[0:n, 5, 256:264], Lf, dtb[0:n, 4, t], start=True, stop=True)
                    if t < 2:
                        m = mm(ps[:, 5, 264:272], onesf, dtb[:, 4, t], start=True, stop=True)
                    else:
                        pe.wait_ge(S("am_done"), l + 1)
                        m = mm(ps[:, 5, 264:264 + NSQ * NH], onesf[0:n], am[0:n].rearrange("p b h -> p (b h)"),
                               start=True, stop=True)
                    m.then_inc(S("w_mm"), 1)
                    pe.wait_ge(S("La_done"), i + 1)
                    if t:
                        pe.wait_ge(S("dec_exp"), 2 * i)
                    for r in range(NH):
                        m = mm(ps[0:n, r // 4, (r % 4) * n:(r % 4 + 1) * n], La[0:n, r, 0:n], Uf, start=True, stop=True)
                    m.then_inc(S("diff_mm"), 1)
                    pe.wait_ge(S("aex_done"), i + 1)
                    if t == 0:
                        pe.wait_ge(S("hg_o"), l + 1)
                        pe.wait_ge(S("sc_done"), LTH(l, 2, 3) + 1)
                    else:
                        pe.wait_ge(S("ssd_y"), i)
                        pe.wait_ge(S("E_exp"), i)
                    for j in range(4):
                        m = mm(ps[:, 2, j * n:(j + 1) * n], aex[0:n, 2 * j:2 * j + 2, :].rearrange("p h d -> p (h d)"), Uf,
                               start=True, stop=True)
                    m.then_inc(S("E_mm"), 1)
                    if t:
                        pe.wait_ge(S("P_done"), 2 * i)
                    for g in range(G):
                        m = mm(ps[0:n, 3, g * n:(g + 1) * n], cvT[:, 4 + g, o:o + n], cvT[:, 6 + g, o:o + n],
                               start=True, stop=True)
                    m.then_inc(S("cb_mm"), 1)
                    if t == 1:
                        pe.wait_ge(S("E_exp"), i + 1)
                        pe.wait_ge(S("ss_done"), 2 * l + 1)
                        for j in range(4):
                            m = mm(ps[:, 2, j * n:(j + 1) * n], SS[:, j * P:(j + 1) * P], cvT[:, 6 + j // 2, o:o + n],
                                   start=True, stop=True)
                        m.then_inc(S("yx_mm"), 1)
                    pe.wait_ge(S("xw_done"), i + 1)
                    pe.wait_ge(S("P_done"), 2 * i + 2)
                    if t == 0:
                        pe.wait_ge(S("o_evac"), LT(l, 2) + 1)
                    for j in range(4):
                        for hh in range(2):
                            r = 2 * j + hh
                            m = mm(ps[hh * HD:(hh + 1) * HD, 6, j * n:(j + 1) * n], xdt[0:n, r * HD:(r + 1) * HD],
                                   M[0:n, r, 0:n], start=True, stop=True)
                    m.then_inc(S("yi_mm"), 1)
                    if t < 2:
                        pe.wait_ge(S("Bt_done"), i + 1)
                        if t == 0:
                            pe.wait_ge(S("kx_exp"), LT(l, 2) + 1)
                        else:
                            pe.wait_ge(S("ss_done"), 2 * l + t)
                        for g in range(G):
                            m = mm(ps[:, 7, 256 * g:256 * g + 256], Bt[0:n, g * P:(g + 1) * P],
                                   xw[0:n, 256 * g:256 * g + 256], start=True, stop=True)
                        m.then_inc(S("hst_mm"), 1)
                pe.wait_ge(S("E_exp"), LT(l, 2) + 1)
                for b in range(NSQ):
                    pe.wait_ge(slab_in[b % 4], 16 * (4 * l + 2 + b // 4 + 1))
                    for j in range(4):
                        m = mm(ps[:, 2, j * NS + b * LSQ:j * NS + (b + 1) * LSQ], slab[:, b % 4, j * P:(j + 1) * P],
                               cvT[:, 6 + j // 2, NPR + b * LSQ:NPR + (b + 1) * LSQ], start=True, stop=True)
                    if b == NSQ - 1:
                        m.then_inc(S("yx_mm"), 1)
                    pe.wait_ge(S("Bm_done"), 8 * l + b + 1)
                    if b >= 2:
                        pe.wait_ge(S("slab_done"), 16 * l + 8 + b - 1)
                    elif b == 0:
                        pe.wait_ge(S("Bt_done"), LT(l, 2) + 1)
                    for g in range(G):
                        m = mm(ps[:, 4 + b % 2, 256 * g:256 * g + 256], Bm[:, b % 2, g * P:(g + 1) * P],
                               xw[0:NS, 256 * g:256 * g + 256], start=True, stop=True)
                    m.then_inc(S("bst_mm"), 1)

                pe.wait_ge(S("gsq_done"), 2 * l + 1)
                pe.wait_ge(S("ssd_y"), 3 * l + 3)
                for h in range(H):
                    mm(ps[:, h, 0:TOK], onesf, sqh[:, h], start=True, stop=True)
                pe.wait_ge(S("gsq_done"), 2 * l + 2)
                pe.wait_ge(S("slab_done"), 16 * l + 16)
                for j in range(4):
                    m = mm(ps[:, 4 + j // 2, 0:TOK], onesf, sqs[:, j], start=j % 2 == 0, stop=j % 2 == 1)
                m.then_inc(S("gss_mm"), 1)
                pe.wait_ge(S("mixL_done"), 2 * l + 2)
                for c in range(2):
                    dense(PLAN["out", l] + 2 * c, c).then_inc(S("used"), 1)

                if l == 0:
                    pe.wait_ge(S("out_evac"), 2)
                    norm_mm(1, sq)
                    pe.wait_ge(S("hnL_done"), 2)
                    for j in range(11):
                        for half in range(2):
                            u = PLAN["up", 0] + 2 * j + half
                            pe.wait_ge(S("split_done"), u + 1)
                            if j >= 2 and half == 0:
                                pe.wait_ge(S("hf_done"), j - 1)
                            wH, wL = unit(u, 8)
                            for i in range(2):
                                for k in range(KT):
                                    m = three(ps[:, 4 * (j % 2) + 2 * half + i, 0:TOK],
                                              (wH[:, k, i * P:(i + 1) * P], wL[:, k, i * P:(i + 1) * P]),
                                              (hnH[:, k], hnL[:, k]), start=k == 0, stop=k == KT - 1)
                            m.then_inc(S("used"), 1)
                    pe.wait_ge(S("hfL_done"), 11)
                    for m_ in range(8):
                        for half in range(2):
                            u = PLAN["down", 0] + 2 * m_ + half
                            pe.wait_ge(S("split_done"), u + 1)
                            wH, wL = unit(u, 11)
                            for k in range(11):
                                kk = 11 * half + k
                                m = three(ps[:, m_, 0:TOK], (wH[:, k], wL[:, k]), (hfH[:, kk], hfL[:, kk]),
                                          start=kk == 0, stop=kk == 21)
                            m.then_inc(S("used"), 1)

            pe.wait_ge(S("out_evac"), 4)
            norm_mm(3, sqm)
            pe.wait_ge(S("hnL_done"), 4)
            for t, (o, n) in enumerate(TILES):
                for k in range(KT):
                    mm(ps[0:n, 1, 8 * t:8 * t + 8], hnH[:, k, o:o + n].bitcast(F32), wro[:, k], start=k == 0, stop=False)
                    m = mm(ps[0:n, 1, 8 * t:8 * t + 8], hnL[:, k, o:o + n].bitcast(F32), wro[:, k],
                           start=False, stop=k == KT - 1)
            m.then_inc(S("lg_mm"), 1)
            for t, (o, n) in enumerate(TILES):
                for q in range(4):
                    k = 4 * t + q
                    if k >= 2:
                        pe.wait_ge(S("tk_done"), k - 1)
                        if (k - 2) % 4 < 2:
                            pe.wait_ge(S("hkL_done"), 2 * ((k - 2) // 4) + (k - 2) % 4 + 1)
                    src = sqm if q < 2 else xT
                    for i in range(4):
                        m = nc.tensor.transpose(ps[0:n, 4 + k % 2, i * P:(i + 1) * P], src[:, 4 * (q % 2) + i, o:o + n], ident)
                    m.then_inc(S("tk_tr"), 1)
            pe.wait_ge(S("routed"), 1)
            for t, (o, n) in enumerate(TILES):
                for tt in range(t + 1):
                    nn = TILES[tt][1]
                    w = tabv("before")[0:nn, 0:n] if tt == t else onesf[0:nn, 0:n]
                    mm(ps[0:n, 1, 32 + 8 * t:40 + 8 * t], w, sml[0:nn, 7, tt], start=tt == 0, stop=tt == t)
            for tt in range(3):
                nn = TILES[tt][1]
                m = mm(ps[:, 1, 64:72], onesf[0:nn], sml[0:nn, 7, tt], start=tt == 0, stop=tt == 2)
            m.then_inc(S("rank_mm"), 1)
            pe.wait_ge(S("rounds_ready"), 1)
            pe.wait_ge(S("hkL_done"), 6)
            pe.wait_ge(S("tk_done"), 12)

            def gather(it):
                pe.wait_ge(S("sel_done"), it + 1)
                for q in range(4):
                    if q >= 2:
                        pe.wait_ge(S("X_done"), it * 4 + (q - 1))
                    src = hkH if q < 2 else hkL
                    for k in range(4):
                        kk = 4 * (q % 2) + k
                        for t, (o, n) in enumerate(TILES):
                            m = mm(ps[:, 2 + q % 2, k * P:(k + 1) * P], src[0:n, t, kk * P:(kk + 1) * P], sel[0:n, t],
                                   start=t == 0, stop=t == 2)
                    m.then_inc(S("gath_mm"), 1)

            def expert_pe(it):
                pe.wait_ge(S("X_done"), it * 4 + 4)
                pe.wait_ge(S("ht_add"), it * 6 + 1)
                for j, (kind, c, i) in enumerate(EXPERT_UNITS):
                    pe.wait_ge(S("split_done"), it * EU + (U0 + j + 1))
                    wH, wL = [x.rearrange("p (k n) -> p k n", k=4 if kind == "up" else 2) for x in esplit(j)]
                    if kind == "up":
                        if i == 0 and c >= 2:
                            pe.wait_ge(S("eh_done"), it * EC + c)
                        for k in range(4):
                            kk = 4 * (i % 2) + k
                            m = three(ps[:, 2 * (c % 2) + i // 2, :], (XH[:, kk], XL[:, kk]), (wH[:, k], wL[:, k]),
                                      start=kk == 0, stop=kk == KT - 1)
                    else:
                        if i == 0:
                            pe.wait_ge(S("hTL_done"), it * EC + (c + 1))
                        for k in range(2):
                            f = 2 * i + k
                            for q in range(2):
                                m = three(ps[:, 6 + q, :], (hTH[:, f], hTL[:, f]),
                                          (wH[:, k, 512 * q:512 * q + 512], wL[:, k, 512 * q:512 * q + 512]),
                                          start=c == 0 and f == 0, stop=c == EC - 1 and f == 3)
                    m.then_inc(S("used"), 1)
                    if j == UP_LAST[0]:
                        for t, (o, n) in enumerate(TILES):
                            m = nc.tensor.transpose(ps[:, 5, o:o + n], sel[0:n, t].bitcast(F32), ident[0:n, 0:n])
                        m.then_inc(S("selT_tr"), 1)
                    if j == UP_LAST[-1]:
                        pe.wait_ge(S("eh_done"), it * EC + EC)
                        gather(it + 1)
                    if j in TURN_AT:
                        c = TURN_AT.index(j)
                        pe.wait_ge(S("eh_done"), it * EC + (c + 2))
                        if c:
                            pe.wait_ge(S("hTL_done"), it * EC + c)
                        for k in range(4):
                            m = nc.tensor.transpose(ps[:, 4, k * P:(k + 1) * P], sg[:, 1, k * P:(k + 1) * P], ident)
                        m.then_inc(S("eh_tr"), 1)
                pe.wait_ge(S("yL_done"), it * 2 + 2)
                pe.wait_ge(S("X_done"), it * 4 + 8)
                for t in range(3):
                    for q in range(2):
                        mm(ps[:, 2 * t + q, :], selT[:, t], yH[:, 512 * q:512 * q + 512], start=True, stop=False)
                        mm(ps[:, 2 * t + q, :], selT[:, t], yL[:, 512 * q:512 * q + 512], start=False, stop=True
                           ).then_inc(S("scat_mm"), 1)

            gather(0)
            with pe.Fori(0, NE) as e:
                expert_pe(e)
            rounds = pe.value_load(rndi[0:1, 0:1], min_val=1, max_val=MAXR)
            with pe.If(rounds > 1):
                with pe.Fori(1, rounds) as r:
                    with pe.Fori(0, NE) as e:
                        expert_pe(pe.snap(r * NE + e))


_INS = ["x_prompt", "x_sample", "state_hgrn", "state_ssm", "state_conv", "norm_mix", "w_in", "conv_w", "conv_b",
        "a_log", "dt_bias", "d_skip", "lb_param", "hg_norm", "ssd_norm", "w_out", "norm_ffn", "w_ffn_in",
        "w_ffn_out", "w_router", "w_exp_in", "w_exp_out", "norm_final"]
_OUTS = [(1, NPR, D), (NSQ, LSQ, D), (DEPTH, 1, H, P, P), (DEPTH, 1, NH, P, HD), (DEPTH, 1, 3, CONV),
         (DEPTH, NSQ, H, P, P), (DEPTH, NSQ, NH, P, HD), (DEPTH, NSQ, 3, CONV)]


def kernel(**inputs):
    import concourse.bacc as _bacc
    from concourse.bass_utils import run_bass_kernel_spmd as _run

    nc = _bacc.Bacc("TRN2", target_bir_lowering=False, num_devices=1)
    arrays, aps = {}, {}
    table, at = constants()
    for name in _INS + ["table"]:
        arr = np.ascontiguousarray(table if name == "table" else inputs[name])
        arrays[f"in_{name}_dram"] = arr
        aps[name] = nc.dram_tensor(f"in_{name}_dram", arr.shape, mybir.dt.from_np(arr.dtype),
                                   kind="ExternalInput").ap()
    outs = [nc.dram_tensor(f"out_{i}_dram", shape, F32, kind="ExternalOutput").ap() for i, shape in enumerate(_OUTS)]
    build(nc, aps, outs, table, at)
    r = _run(nc, [arrays], core_ids=[0])
    return tuple(r.results[0][f"out_{i}_dram"] for i in range(len(_OUTS)))
```

```python
from contextlib import ExitStack

import numpy as np

import concourse.bass as bass
from concourse import mybir

F32 = mybir.dt.float32
F32R = mybir.dt.float32r
I32 = mybir.dt.int32
ACT = mybir.ActivationFunctionType
ALU = mybir.AluOpType
AX = mybir.AxisListType

P = 128
D = 1024
KT = D // P
NPR, NSQ, LSQ = 256, 8, 8
NS = NSQ * LSQ
TOK = NPR + NS
TILES = [(0, 128), (128, 128), (256, 64)]
DEPTH = 2
H = 4
NH, HD, G = 8, 64, 2
CONV = 1024
TAPS = 4
PADC = (TAPS - 1) + NPR + NSQ * (TAPS - 1 + LSQ)
NIN = 3592
DFF, DFE, NE = 2816, 3584, 8
EPS = 1e-6
CAP = 128
MAXR = -(-TOK // CAP)

LV = 7
LS = 3
RING = 6
UN = 2048


def level_tables(n, levels, seq):
    i = np.arange(n)
    same = (i[:, None] // seq) == (i[None, :] // seq)
    w = np.zeros((n, levels + 1, n), np.float32)
    m = np.zeros((n, levels + 1, n), np.float32)
    for v in range(levels):
        b = 1 << v
        for t in range(n):
            ref = (t // (2 * b)) * 2 * b + b - 1
            if t > ref:
                w[ref + 1:t + 1, v, t] = 1
            else:
                w[t + 1:ref + 1, v, t] = 1
        left = (i // b) % 2 == 0
        pair = (i[:, None] // (2 * b)) == (i[None, :] // (2 * b))
        m[:, v, :] = pair & left[:, None] & ~left[None, :]
    w[:, levels, :] = same & (i[:, None] <= i[None, :])
    m[:, levels, :] = np.eye(n)
    after = (same & (i[:, None] > i[None, :])).astype(np.float32)
    return w, after, m


def constants():
    wp, lp, mp = level_tables(128, LV, 128)
    ws, ls, ms = level_tables(NS, LS, LSQ)
    i = np.arange(P)
    seq = ((i[:, None] // LSQ) == np.arange(NSQ)[None, :]).astype(np.float32)
    lspad = np.zeros((NS, P), np.float32)
    lspad[:, :NS] = ls
    parts = {
        "w": wp.reshape(P, -1), "l": lp, "ws": ws.reshape(NS, -1), "ls": lspad,
        "id": np.eye(P), "ones": np.ones((P, P)), "mask": mp.reshape(P, -1), "ms": ms.reshape(NS, -1), "seq": seq,
        "iota": np.tile(i[None, :], (P, 1)), "before": (i[:, None] < i[None, :]),
    }
    at, n = {}, 0
    for k, v in parts.items():
        at[k] = (n, v.shape[1])
        n += v.shape[1]
    out = np.zeros((P, n), np.float32)
    for k, v in parts.items():
        out[:v.shape[0], at[k][0]:at[k][0] + v.shape[1]] = v
    return out, at


def unit_plan():
    u, plan = 0, {}
    for l in range(DEPTH):
        plan["in", l] = u
        u += 14
        plan["out", l] = u
        u += 4
        if l % 2 == 0:
            plan["up", l] = u
            u += 22
            plan["down", l] = u
            u += 16
        else:
            plan["moe", l] = u
    return plan


PLAN = unit_plan()
CHUNKS = [2560, 3072, 0, 1536, 2048, 512, 1024]
C_XS, C_BC, C_Q, C_OG, C_Z, C_F, C_I = range(7)
EC = DFE // 512
EXPERT_UNITS = [("up", 0, i) for i in range(4)]
for _c in range(1, EC):
    EXPERT_UNITS += [("up", _c, i) for i in range(4)] + [("down", _c - 1, i) for i in range(2)]
EXPERT_UNITS += [("down", EC - 1, i) for i in range(2)]
EU = len(EXPERT_UNITS)
HG_BANKS = (0, 1, 3, 7)
AHEAD = 3
ERING = 7
assert EU % AHEAD == 0 and EU % ERING == 0
UP_LAST = [EXPERT_UNITS.index(("up", c, 3)) for c in range(EC)]
TURN_AT = [EXPERT_UNITS.index(("up", c + 1, 1)) for c in range(EC - 1)] + [EXPERT_UNITS.index(("down", EC - 2, 1))]


def build(nc, a, outs, table, at):
    y_prompt, y_sample, hg_p, ssm_p, conv_p, hg_s, ssm_s, conv_s = outs
    ctx = ExitStack()
    with ctx:
        base = nc.sbuf_base
        room = nc.sbuf_usable_end - base - 64
        base = -(-base // 64) * 64
        fence = ctx.enter_context(nc.sbuf_tensor("fence", [P, (room - 64) // 4], F32))
        cursor = [base]

        def put(name, shape, dt=F32, offset=None):
            size = 4 * int(np.prod(shape[1:]))
            if offset is None:
                offset = cursor[0]
                cursor[0] = offset + -(-size // 32) * 32
                assert cursor[0] <= base + room - 128, (name, cursor[0] - base, room)
            return nc.alloc_sbuf_tensor_at(name, shape, dt, offset=offset)

        xT = put("xT", [P, KT, TOK])
        hnH = put("hnH", [P, KT, TOK], F32R)
        hnL = put("hnL", [P, KT, TOK], F32R)
        ring = put("ring", [P, RING, UN])
        spH = put("spH", [P, 2, UN], F32R)
        spL = put("spL", [P, 2, UN], F32R)
        nr = at["id"][0]
        tabR = put("tabR", [P, nr], F32R)
        tab = put("tab", [P, table.shape[1] - nr])
        vec = put("vec", [P, DEPTH, 68])
        wnH = put("wnH", [P, DEPTH + 1, KT, NH], F32R)
        wnL = put("wnL", [P, DEPTH + 1, KT, NH], F32R)
        bc = put("bc", [P, DEPTH, 3, NH])
        eps = put("eps", [P, 1])
        lbom = put("lbom", [P, DEPTH, 2, H])
        lbt = put("lbt", [P, 4, H])
        arena = cursor[0]

        def tabv(name, dt=F32):
            o, n = at[name]
            if o < nr:
                v = tabR[:, o:o + n]
                return v if dt == F32R else v.bitcast(F32)
            return tab[:, o - nr:o - nr + n]

        ident = tabv("id")
        onesf = tabv("ones")

        cursor[0] = arena
        qT = put("qT", [P, H, TOK])
        kT = put("kT", [P, H, TOK])
        lfT = put("lfT", [P, H, TOK])
        oT = put("oT", [P, H, TOK])
        ogT = put("ogT", [P, H, TOK])
        zT = put("zT", [P, H, TOK])
        cvT = put("cvT", [P, 8, TOK])
        tok0 = cursor[0]
        lfH = put("lfH", [P, H * P], F32R)
        lfL = put("lfL", [P, H * P], F32R)
        kd = put("kd", [P, H * P])
        vtk = put("vtk", [P, H * P])
        xdt = put("xdt", [P, NH * HD])
        xw = put("xw", [P, NH * HD])
        Bt = put("Bt", [P, G * P])
        SH = put("SH", [P, H * P])
        rstd = put("rstd", [P, TOK], offset=cursor[0] - 4 * H * P)
        SS = put("SS", [P, NH * HD])
        kdm_at = cursor[0]
        kdm = put("kdm", [NS, 4, H * P])
        ov = cursor[0]
        M = put("M", [P, LV + 1, P])
        Yq = put("Yq", [P, LV + 1, P])
        Yk = put("Yk", [P, LV, P])
        sc0 = cursor[0]
        SC = put("SC", [P, LV + 1, P])
        qG = put("qG", [P, H, NS])
        egl = put("egl", [P, H, NSQ])
        dtb = put("dtb", [P, 5, 3, NH])
        wsm = put("wsm", [P, NH])
        xbc = put("xbc", [P, 8, PADC], offset=ov)
        cvt = put("cvt", [P, 2, PADC], offset=sc0)
        cst = put("cst", [NSQ * 3, CONV], offset=tok0)
        cpk = put("cpk", [P, 8, 3 + NSQ * 3], offset=tok0 + 4 * CONV)
        cso = put("cso", [3 + NSQ * 3, CONV], offset=tok0 + 8 * CONV)
        Bm = put("Bm", [NS, NSQ, G * P], offset=tok0 + 17 * 1024)
        dtT = put("dtT", [NH, TOK], offset=tok0 + 15 * 1024)
        assert kdm_at == tok0 + 17 * 1024
        hn0 = base + 4 * KT * TOK
        Mb = [M, put("M1", [P, LV + 1, P], offset=hn0)]
        Yqb = [Yq, put("Yq1", [P, LV + 1, P], offset=hn0 + 4 * 1024)]
        Ykb = [Yk, put("Yk1", [P, LV, P], offset=hn0 + 8 * 1024)]
        ea = put("ea", [P, NSQ * NH], offset=hn0 + 16 * 1024)
        am = put("am", [P, NSQ, NH], offset=hn0 + 17 * 1024)
        SCb = [SC, put("SC1", [P, LV + 1, P], offset=hn0 + 12 * 1024)]
        La = put("La", [P, NH, P], offset=ov + 4 * 1024)
        t1 = put("t1", [P, 4, P], offset=ov + 8 * 1024)
        CBm = put("CBm", [P, G, P], offset=tok0)
        aex = put("aex", [P, NH, HD], offset=sc0)
        EE = put("EE", [P, 4, P], offset=sc0 + 4 * 512)
        sq = put("sq", [P, KT, TOK], offset=arena)
        xin = put("xin", [P, 3, D], offset=arena + 4 * KT * TOK)
        vin = put("vin", [68, DEPTH, P], offset=arena + 4 * (KT * TOK + 3 * D))
        sqh = put("sqh", [P, H, TOK], offset=arena)
        sqs = put("sqs", [P, 4, TOK], offset=arena + 4 * H * TOK)
        rsh = put("rsh", [P, H, TOK], offset=arena + 8 * H * TOK)
        rss = put("rss", [P, G, TOK], offset=ov)
        wnr = put("wnr", [P, DEPTH + 1, KT, NH], offset=tok0 + 24 * 1024)
        stage = put("stage", [P, nr], offset=tok0 + 17 * 1024)

        NF = DFF // P
        cursor[0] = arena + 4 * KT * TOK
        hfH = put("hfH", [P, NF, TOK], F32R)
        hfL = put("hfL", [P, NF, TOK], F32R)
        gs = put("gs", [P, 2, TOK])
        hf = put("hf", [P, 2, TOK])

        cursor[0] = arena
        hk = put("hk", [P, 3, D])
        fsq = put("fsq", [P, 3, D])
        ht = put("ht", [P, 3, D])
        yH = put("yH", [P, D], F32R)
        yL = put("yL", [P, D], F32R)
        sg = put("sg", [P, 2, 512])
        hTH = put("hTH", [P, 4, P], F32R)
        hTL = put("hTL", [P, 4, P], F32R)
        sel = put("sel", [P, 3, P], F32R)
        selT = put("selT", [P, 3, P], F32R)
        sml = put("sml", [P, 12, 3, NE])
        rank = put("rank", [P, NE + 1, 3])
        gate = put("gate", [P, NE, 3])
        rk = put("rk", [P, 2, 3])
        rnd = put("rnd", [P, 4])
        rndi = put("rndi", [P, 1], I32)
        ring6 = put("ring6", [P, 1, UN])
        spH2 = put("spH2", [P, 1, UN], F32R)
        spL2 = put("spL2", [P, 1, UN], F32R)
        sqm = put("sqm", [P, KT, TOK], offset=arena + 4 * 9 * D)
        gfin = put("gfin", [P, D], offset=arena)
        fss = put("fss", [P, 4], offset=arena + 4 * D)
        XH = put("XH", [P, KT, P], F32R, offset=base + 4 * KT * TOK)
        XL = put("XL", [P, KT, P], F32R, offset=base + 8 * KT * TOK)

        ps = ctx.enter_context(nc.psum_tensor("ps", [P, 8, 512], F32))

        sems = {}

        def S(name):
            if name not in sems:
                sems[name] = ctx.enter_context(nc.semaphore(name))
            return sems[name]

        landed = [S(f"landed{i}") for i in range(RING + 1)]
        slab_in = [S(f"slab_in{i}") for i in range(4)]

        U0 = PLAN["moe", 1]

        def eslot(j):
            i = j % ERING
            if i == ERING - 1:
                return ring6[:, 0], landed[RING], 0
            q = (U0 + i) % RING
            return ring[:, q], landed[q], len(range(q, U0, RING))

        def esplit(j):
            i = j % AHEAD
            return (spH2[:, 0], spL2[:, 0]) if i == 2 else (spH[:, i], spL[:, i])

        def raw(u, n=UN):
            return ring[:, u % RING, 0:n]

        def slab(l, k):
            return ring[:, (PLAN["out", l] + 4 + k // 4) % RING, 512 * (k % 4):512 * (k % 4) + 512]

        def unit_src(u):
            for l in range(DEPTH):
                i = u - PLAN["in", l]
                if 0 <= i < 14:
                    c, h = divmod(i, 2)
                    src = a["w_in"][l, h * 512:(h + 1) * 512, CHUNKS[c]:CHUNKS[c] + 512]
                    return src.rearrange("(k p) n -> p k n", p=P), UN, 4
                i = u - PLAN["out", l]
                if 0 <= i < 4:
                    c, h = divmod(i, 2)
                    src = a["w_out"][l, h * 512:(h + 1) * 512, c * 512:(c + 1) * 512]
                    return src.rearrange("(k p) n -> p k n", p=P), UN, 4
            i = u - PLAN["up", 0]
            if 0 <= i < 22:
                j, h = divmod(i, 2)
                c0 = h * DFF + j * 256
                return a["w_ffn_in"][0, :, c0:c0 + 256].rearrange("(k p) n -> p k n", p=P), UN, 8
            i = u - PLAN["down", 0]
            m, h = divmod(i, 2)
            src = a["w_ffn_out"][0, h * 1408:(h + 1) * 1408, m * P:(m + 1) * P]
            return src.rearrange("(k p) n -> p k n", p=P), 1408, 11

        def LT(l, t):
            return l * 3 + t

        def LTH(l, t, h):
            return (l * 3 + t) * H + h

        def vectors(queue, l):
            r = 0
            for src, k in ((a["norm_mix"][l], 8), (a["norm_ffn"][l], 8), (a["conv_b"][l], 8),
                           (a["conv_w"][l].rearrange("t c -> (t c)"), 32), (a["hg_norm"][l], 4),
                           (a["ssd_norm"][l], 4), (a["lb_param"][l], 4)):
                queue.dma_start(vin[r:r + k, l], src.rearrange("(k p) -> k p", p=P)).then_inc(S(f"vec_in{l}"), 16)
                r += k

        block = ctx.enter_context(nc.Block())

        @block.sync
        def _(sp):
            def slab_dma_views(l, k, tensors):
                view = slab(l, k).rearrange("p (h v) -> p h v", h=H if k < 8 else NH)
                if k < 8:
                    return tensors[0][l, k].rearrange("h k v -> k h v"), view
                return tensors[1][l, k - 8].rearrange("h n p -> n h p"), view

            def states(l):
                for k in range(16):
                    if k % 4 == 0:
                        sp.wait_ge(S("split_done"), PLAN["out", l] + 4 + k // 4 - RING + 1)
                    src, view = slab_dma_views(l, k, (a["state_hgrn"], a["state_ssm"]))
                    sp.dma_start(view, src).then_inc(slab_in[k // 4], 16)
                for k in range(16):
                    sp.wait_ge(S("slab_done"), l * 16 + k + 1)
                    dst, view = slab_dma_views(l, k, (hg_s, ssm_s))
                    sp.dma_start(dst, view).then_inc(S("slab_out"), 16)
                sp.wait_ge(S("slab_out"), 16 * 16 * (l + 1))

            for t, (o, n) in enumerate(TILES):
                src = a["x_prompt"][0, o:o + n] if t < 2 else a["x_sample"].rearrange("b s d -> (b s) d")
                sp.dma_start(xin[0:n, t], src).then_inc(S("x_in"), 16)
            small = nr + 2 * P
            for u in range(PLAN["moe", 1]):
                if u == 2:
                    sp.dma_start(stage[:], a["table"][:, 0:nr]).then_inc(S("stage_in"), 16)
                    sp.dma_start(tab[:, 2 * P:], a["table"][:, small:]).then_inc(S("tab_in"), 16)
                src, n, k = unit_src(u)
                if u >= RING:
                    sp.wait_ge(S("split_done"), u - RING + 1)
                dst = raw(u, n).rearrange("p (k n) -> p k n", k=k)
                sp.dma_start(dst, src).then_inc(landed[u % RING], 16)
                for l in range(DEPTH):
                    if u == PLAN["out", l] + 3:
                        states(l)

            w1, w2 = a["w_exp_in"][0], a["w_exp_out"][0]

            def expert_load(e, it, j):
                kind, c, i = EXPERT_UNITS[j % EU]
                dst, sem, _ = eslot(j)
                if kind == "up":
                    c0 = (i // 2) * DFE + c * 512
                    src, k = w1[bass.ds(e, 1), (i % 2) * 512:(i % 2) * 512 + 512, c0:c0 + 512], 4
                else:
                    row = c * 512 + i * 256
                    src, k = w2[bass.ds(e, 1), row:row + 256, :], 2
                sp.wait_ge(S("split_done"), it * EU + (U0 + j - ERING + 1))
                sp.dma_start(dst.rearrange("p (k n) -> p k n", k=k),
                             src.rearrange("e (k p) n -> p (e k) n", p=P)).then_inc(sem, 16)

            def expert_loads(e, it):
                now = sp.snap(e)
                then = sp.snap((e + 1) % NE)
                for j in range(AHEAD, EU + AHEAD):
                    expert_load(now if j < EU else then, it, j)

            sp.wait_ge(S("split_done"), U0)
            for j in range(AHEAD):
                expert_load(0, 0, j)
            sp.wait_ge(S("out_evac"), 2 * DEPTH)
            sp.wait_ge(S("mixer_stored"), DEPTH)
            with sp.Fori(0, NE) as e:
                expert_loads(e, e)
            sp.wait_ge(S("rounds_ready"), 1)
            rounds = sp.value_load(rndi[0:1, 0:1], min_val=1, max_val=MAXR)
            with sp.If(rounds > 1):
                with sp.Fori(1, rounds) as r:
                    with sp.Fori(0, NE) as e:
                        expert_loads(e, sp.snap(r * NE + e))
        @block.gpsimd
        def _(pool):
            nc.gpsimd.memset(eps[:], EPS).then_inc(S("eps_set"), 1)
            vectors(pool, 1)
            for l in range(DEPTH):
                pool.dma_start(wnr[:, l], a["w_in"][l, :, NIN - NH:NIN].rearrange("(k p) n -> p k n", p=P)
                               ).then_inc(S("small_in"), 16)
                pool.dma_start(bc[:, l, 0], a["dt_bias"][l].partition_broadcast(P)).then_inc(S("small_in"), 16)
                pool.dma_start(bc[:, l, 1], a["a_log"][l].partition_broadcast(P)).then_inc(S("small_in"), 16)
                pool.dma_start(bc[:, l, 2], a["d_skip"][l].partition_broadcast(P)).then_inc(S("small_in"), 16)
            pool.dma_start(wnr[:, DEPTH], a["w_router"][0].rearrange("(k p) n -> p k n", p=P)).then_inc(S("small_in"), 16)

            for l in range(DEPTH):
                if l:
                    pool.wait_ge(S("used"), PLAN["in", l])
                pool.dma_start(cst[:], a["state_conv"][l].rearrange("b r c -> (b r) c")).then_inc(S("cst_in"), 16)
                nc.gpsimd.memset(xbc[:, :, 0:3], 0.0).then_inc(S("pad_zero"), 1)
                pool.wait_ge(S("cso_done"), 2 * l + 2)
                pool.dma_start(conv_p[l, 0], cso[0:3, :]).then_inc(S("conv_stored"), 16)
                pool.dma_start(conv_s[l].rearrange("b r c -> (b r) c"), cso[3:27, :]).then_inc(S("conv_stored"), 16)

                pool.wait_ge(S("sh_done"), 2 * l + 2)
                pool.dma_start(hg_p[l, 0].rearrange("h k v -> k h v"),
                               SH[:].rearrange("p (h v) -> p h v", h=H)).then_inc(S("hgp_stored"), 16)
                for b in range(NSQ):
                    if b == 0:
                        pool.wait_ge(S("tab_in"), 16)
                        pool.wait_ge(S("kd_done"), LT(l, 2) + 1)
                    if b >= 4:
                        pool.wait_ge(S("sst_mm"), l * 8 + b - 3)
                    nc.gpsimd.tensor_scalar(kdm[:, b % 4], kd[0:NS], tabv("seq")[0:NS, b:b + 1], None, ALU.mult
                                            ).then_inc(S("kdm_done"), 1)
                for b in range(NSQ):
                    if b == 0:
                        pool.wait_ge(S("Bt_done"), LT(l, 2) + 1)
                        pool.wait_ge(S("sst_mm"), l * 8 + 8)
                    nc.gpsimd.tensor_scalar(Bm[:, b], Bt[0:NS], tabv("seq")[0:NS, b:b + 1], None, ALU.mult
                                            ).then_inc(S("Bm_done"), 1)
                pool.wait_ge(S("ss_done"), 2 * l + 2)
                pool.dma_start(ssm_p[l, 0].rearrange("h n p -> n h p"),
                               SS[:].rearrange("p (h v) -> p h v", h=NH)).then_inc(S("ssp_stored"), 16)
                pool.wait_ge(S("conv_stored"), 32 * (l + 1))
                pool.wait_ge(S("hgp_stored"), 16 * (l + 1))
                pool.wait_ge(S("ssp_stored"), 16 * (l + 1))
                pool.sem_inc(S("mixer_stored"), 1)

            pool.wait_ge(S("moe_sum"), 1)
            pool.dma_start(gfin[:], a["norm_final"].partition_broadcast(P)).then_inc(S("gfin_in"), 16)
            for t, (o, n) in enumerate(TILES):
                pool.wait_ge(S("y_done"), t + 1)
                dst = y_prompt[0, o:o + n] if t < 2 else y_sample.rearrange("b s d -> (b s) d")
                pool.dma_start(dst, ht[0:n, t]).then_inc(S("y_out"), 16)
            pool.wait_ge(S("y_out"), 48)

        @block.scalar
        def _(act):
            A = nc.scalar.activation
            steps = [0]

            def own(ins):
                steps[0] += 1
                ins.then_inc(S("act_step"), 1)
                act.wait_ge(S("act_step"), steps[0])

            def split_hi(u, n=UN):
                if u >= PLAN["down", 0] and u < PLAN["in", 1]:
                    n = 1408
                act.wait_ge(landed[u % RING], 16 * (u // RING + 1))
                if u >= 2:
                    act.wait_ge(S("used"), u - 1)
                A(spH[:, u % 2, 0:n], raw(u, n), ACT.Copy).then_inc(S("hi_done"), 1)

            def norm_t(k, src_ready, val, sqv, before_rstd=()):
                act.wait_ge(src_ready, val)
                A(sqv[:, 0:4], xT[:, 0:4], ACT.Square).then_inc(S("sq_done"), 1)
                for u in before_rstd:
                    split_hi(u)
                if k == 1:
                    act.wait_ge(S("mixer_stored"), 1)
                act.wait_ge(S("ss_mm"), k + 1)
                if k == 0:
                    act.wait_ge(S("eps_set"), 1)
                own(A(rstd[:], ps[:, 0, 0:TOK], ACT.Ln, bias=eps[:, 0:1], scale=1.0 / D))
                A(rstd[:], rstd[:], ACT.Exp, scale=-0.5).then_inc(S("rstd_done"), 1)
                for half in range(2):
                    act.wait_ge(S("hn_f"), 2 * k + half + 1)
                    A(hnH[:, 4 * half:4 * half + 4], sqv[:, 4 * half:4 * half + 4], ACT.Copy
                      ).then_inc(S("hnH_done"), 1)

            act.dma_start(tab[:, 0:2 * P], a["table"][:, nr:nr + 2 * P]).then_inc(S("id_in"), 16)
            vectors(act, 0)
            for t, (o, n) in enumerate(TILES):
                for half in range(2):
                    i = 2 * t + half
                    act.wait_ge(S("xin_tr"), i + 1)
                    A(xT[:, 4 * half:4 * half + 4, o:o + n],
                      ps[:, 2 + i % 2, 0:4 * n].rearrange("p (k n) -> p k n", k=4), ACT.Copy
                      ).then_inc(S("xT_done"), 1)

            for l in range(DEPTH):
                u = PLAN["in", l]
                if l == 0:
                    norm_t(0, S("xT_done"), 5, sq, (u, u + 1))
                    act.wait_ge(S("small_in"), 16 * (4 * DEPTH + 1))
                    A(bc[:, :, 1], bc[:, :, 1], ACT.Exp).then_inc(S("aexp_done"), 1)
                    A(wnH[:], wnr[:], ACT.Copy).then_inc(S("wn_hi"), 1)
                    act.wait_ge(S("lb_max"), 1)
                    A(lbt[:, 0:2], lbt[:, 0:2], ACT.Exp).then_inc(S("lb_exp"), 1)
                else:
                    norm_t(2, S("down_evac"), 4, sq, (u, u + 1))
                if l == 0:
                    act.wait_ge(S("stage_in"), 16)
                    A(tabR[:], stage[:], ACT.Copy).then_inc(S("tab_round"), 1)
                act.wait_ge(S("cst_tr"), l + 1)
                for k in range(8):
                    dst = xbc[:, k, 3 + NPR:PADC].rearrange("p (b r) -> p b r", b=NSQ)[:, :, 0:3]
                    A(dst, ps[:, 6, 24 * k:24 * k + 24].rearrange("p (b r) -> p b r", b=NSQ), ACT.Copy
                      ).then_inc(S("pads_done"), 1)
                for c in range(7):
                    split_hi(u + 2 * c + 2)
                    split_hi(u + 2 * c + 3)
                    if c == C_F:
                        act.wait_ge(S("fz_done"), l + 1)
                        own(A(kT[:], lfT[:], ACT.Exp, scale=-1.0))
                        own(A(lfT[:], kT[:], ACT.Ln, bias=1.0))
                        A(lfT[:], lfT[:], ACT.Exp, scale=-1.0).then_inc(S("sigm_done"), 1)
                        act.wait_ge(S("dt_abs"), l + 1)
                        own(A(dtb[:, 2], dtb[:, 1], ACT.Exp, scale=-1.0))
                        A(dtb[:, 2], dtb[:, 2], ACT.Ln, bias=1.0).then_inc(S("dt_ln"), 1)
                        act.wait_ge(S("k_done"), l + 1)
                        act.wait_ge(S("lb_done"), 1)
                        for h in range(H):
                            A(lfT[:, h], lfT[:, h], ACT.Ln, bias=lbom[:, l, 0, h:h + 1],
                              scale=lbom[:, l, 1, h:h + 1]).then_inc(S("lf_done"), 1)
                        continue
                    act.wait_ge(S("used"), u + 2 * c + 2)
                    bank = 4 * (c % 2)
                    src = ps[:, bank:bank + 4, 0:TOK]
                    if c in (C_XS, C_BC):
                        m = 4 * c
                        A(xbc[:, m:m + 4, 3:3 + NPR], src[:, :, 0:NPR], ACT.Copy)
                        for k in range(4):
                            dst = xbc[:, m + k, 3 + NPR:PADC].rearrange("p (b r) -> p b r", b=NSQ)[:, :, 3:]
                            ins = A(dst, src[:, k, NPR:TOK].rearrange("p (b r) -> p b r", b=NSQ), ACT.Copy)
                        ins.then_inc(S("proj_evac"), 1)
                    elif c in (C_Q, C_OG, C_Z):
                        A({C_Q: qT, C_OG: ogT, C_Z: zT}[c][:], src, ACT.Silu).then_inc(S("proj_evac"), 1)
                    else:
                        A(oT[:], src, ACT.Copy).then_inc(S("proj_evac"), 1)
                    if c in (C_XS, C_BC):
                        for k in range(4 * c, 4 * c + 4):
                            act.wait_ge(S("conv_sum"), 8 * l + k + 1)
                            A(cvT[:, k, 0:NPR], cvt[:, k % 2, 0:NPR], ACT.Silu)
                            A(cvT[:, k, NPR:TOK].rearrange("p (b r) -> p b r", b=NSQ),
                              cvt[:, k % 2, 3 + NPR:PADC].rearrange("p (b r) -> p b r", b=NSQ)[:, :, 0:LSQ],
                              ACT.Silu).then_inc(S("conv_done"), 1)
                for half in range(2):
                    act.wait_ge(S("cso_tr"), 2 * l + half + 1)
                    A(cso[:, 512 * half:512 * half + 512], ps[0:27, 2 + half, :], ACT.Copy
                      ).then_inc(S("cso_done"), 1)

                for t, (o, n) in enumerate(TILES):
                    i = LT(l, t)
                    act.wait_ge(S("lf_tr"), i + 1)
                    A(lfH[0:n], ps[0:n, 4, :], ACT.Copy).then_inc(S("lfH_done"), 1)
                    act.wait_ge(S("kx_mm"), i + 1)
                    A(kd[0:n], ps[0:n, 7, :], ACT.Exp).then_inc(S("kx_exp"), 1)
                    act.wait_ge(S("v_tr"), i + 1)
                    A(vtk[0:n], ps[0:n, 4, :], ACT.Copy).then_inc(S("v_done"), 1)
                    for h in range(H):
                        j = LTH(l, t, h)
                        act.wait_ge(S("x_mm"), j + 1)
                        if j >= 2:
                            act.wait_ge(S("y_done2"), j - 1)
                        M = Mb[h % 2]
                        if t < 2:
                            A(M[:].rearrange("p v n -> p (v n)"), ps[:, 0:2, :].rearrange("p b n -> p (b n)"),
                              ACT.Exp).then_inc(S("x_exp"), 1)
                        else:
                            A(M[:].rearrange("p v n -> p (v n)")[:, 0:(LS + 1) * n], ps[:, 0, 0:(LS + 1) * n],
                              ACT.Exp).then_inc(S("x_exp"), 1)
                    act.wait_ge(S("o_mm"), H * (i + 1))
                    A(oT[:, :, o:o + n], ps[:, 6, 0:H * n].rearrange("p (h n) -> p h n", h=H), ACT.Copy
                      ).then_inc(S("o_evac"), 1)

                for t, (o, n) in enumerate(TILES):
                    i = LT(l, t)
                    act.wait_ge(S("w_mm"), i + 1)
                    if t:
                        act.wait_ge(S("xw_done"), i)
                        act.wait_ge(S("ss_done"), 2 * l + t)
                    A(wsm[0:n], ps[0:n, 5, 256:264], ACT.Exp).then_inc(S("w_exp"), 1)
                    ne = NH if t < 2 else NSQ * NH
                    A(ea[:, 0:ne], ps[:, 5, 264:264 + ne], ACT.Exp).then_inc(S("ea_exp"), 1)
                    A(Bt[0:n], ps[0:n, 5, 0:256], ACT.Copy).then_inc(S("Bt_done"), 1)
                    act.wait_ge(S("diff_mm"), i + 1)
                    if t == 0:
                        act.wait_ge(S("y_done2"), LTH(l, 2, 3) + 1)
                    else:
                        act.wait_ge(S("yi_mm"), i)
                    for g in range(2):
                        A(Mb[0][0:n, 4 * g:4 * g + 4, 0:n], ps[0:n, g, 0:4 * n].rearrange("p (r n) -> p r n", r=4),
                          ACT.Exp).then_inc(S("dec_exp"), 1)
                    act.wait_ge(S("E_mm"), i + 1)
                    if t:
                        act.wait_ge(S("ssd_y"), i)
                    A(EE[:, :, 0:n], ps[:, 2, 0:4 * n].rearrange("p (j n) -> p j n", j=4), ACT.Exp
                      ).then_inc(S("E_exp"), 1)

                act.wait_ge(S("hg_o"), l + 1)
                A(sqh[:], oT[:], ACT.Square).then_inc(S("gsq_done"), 1)
                act.wait_ge(S("gss_mm"), 2 * l + 1)
                for h, bank in enumerate(HG_BANKS):
                    ins = A(rsh[:, h], ps[:, bank, 0:TOK], ACT.Ln, bias=eps[:, 0:1], scale=1.0 / P)
                own(ins)
                A(rsh[:], rsh[:], ACT.Exp, scale=-0.5).then_inc(S("grs_done"), 1)
                act.wait_ge(S("mixed_f"), 2 * l + 1)
                A(hnH[:, 0:4], oT[:], ACT.Copy).then_inc(S("mixH_done"), 1)
                act.wait_ge(S("z_done"), l + 1)
                A(sqs[:], cvT[:, 0:4], ACT.Square).then_inc(S("gsq_done"), 1)
                act.wait_ge(S("gss_mm"), 2 * l + 2)
                own(A(rss[:], ps[:, 4:6, 0:TOK], ACT.Ln, bias=eps[:, 0:1], scale=0.5 / P))
                A(rss[:], rss[:], ACT.Exp, scale=-0.5).then_inc(S("grs_done"), 1)
                act.wait_ge(S("mixed_f"), 2 * l + 2)
                A(hnH[:, 4:8], cvT[:, 0:4], ACT.Copy).then_inc(S("mixH_done"), 1)
                uo = PLAN["out", l]
                for k in (2, 3):
                    split_hi(uo + k)
                if l == 0:
                    norm_t(1, S("out_evac"), 1, sq, (uo + 4, uo + 5))
                    uu, ud = PLAN["up", 0], PLAN["down", 0]
                    for j in range(11):
                        split_hi(uu + 2 * j + 2)
                        split_hi(uu + 2 * j + 3)
                        act.wait_ge(S("used"), uu + 2 * j + 2)
                        if j:
                            act.wait_ge(S("hf_done"), j)
                        bank = 4 * (j % 2)
                        A(gs[:], ps[:, bank:bank + 2, 0:TOK], ACT.Silu).then_inc(S("gs_done"), 1)
                        act.wait_ge(S("hf_done"), j + 1)
                        A(hfH[:, 2 * j:2 * j + 2], hf[:], ACT.Copy).then_inc(S("hfH_done"), 1)
                    for m in range(7):
                        split_hi(ud + 2 * m + 2)
                        split_hi(ud + 2 * m + 3)

            act.wait_ge(S("mixer_stored"), 2)
            norm_t(3, S("out_evac"), 3, sqm)
            for t, (o, n) in enumerate(TILES):
                for q in range(4):
                    k = 4 * t + q
                    act.wait_ge(S("tk_tr"), k + 1)
                    dst = hk if q < 2 else ht
                    A(dst[0:n, t, 512 * (q % 2):512 * (q % 2) + 512], ps[0:n, 4 + k % 2, :], ACT.Copy
                      ).then_inc(S("tk_done"), 1)
            act.wait_ge(S("rt_diff"), 1)
            A(sml[:, 9, :, 0:1], sml[:, 8, :, 0:1], ACT.Exp).then_inc(S("rt_exp"), 1)

            def expert_hi(it, j):
                src, sem, before = eslot(j)
                act.wait_ge(sem, it * (16 * EU // ERING) + 16 * (before + j // ERING + 1))
                act.wait_ge(S("used"), it * EU + (U0 + j - AHEAD + 1))
                A(esplit(j)[0], src, ACT.Copy).then_inc(S("hi_done"), 1)

            def gathered(it):
                for q in range(2):
                    act.wait_ge(S("gath_mm"), it * 2 + (q + 1))
                    A(XH[:, 4 * q:4 * q + 4],
                      ps[:, 2 + q, :].rearrange("p (k n) -> p k n", k=4), ACT.Copy).then_inc(S("X_done"), 1)

            def expert_act(it):
                for p in range(EU):
                    if p in UP_LAST:
                        c = UP_LAST.index(p)
                        act.wait_ge(S("used"), it * EU + (U0 + p + 1))
                        act.wait_ge(S("eh_done"), it * EC + (c + 1))
                        A(sg[:, 0], ps[:, 2 * (c % 2), :], ACT.Silu).then_inc(S("sg_done"), 1)
                    if p in TURN_AT:
                        c = TURN_AT.index(p)
                        act.wait_ge(S("eh_tr"), it * EC + (c + 1))
                        A(hTH[:], ps[:, 4, :].rearrange("p (k n) -> p k n", k=4), ACT.Copy
                          ).then_inc(S("hTH_done"), 1)
                    expert_hi(it, p + AHEAD)
                    if p == UP_LAST[-1]:
                        gathered(it + 1)
                act.wait_ge(S("used"), it * EU + (U0 + EU))
                for q in range(2):
                    A(yH[:, 512 * q:512 * q + 512], ps[:, 6 + q, :], ACT.Copy).then_inc(S("yH_done"), 1)

            for j in range(AHEAD):
                expert_hi(0, j)
            gathered(0)
            with act.Fori(0, NE) as e:
                expert_act(e)
            act.wait_ge(S("rounds_ready"), 1)
            rounds = act.value_load(rndi[0:1, 0:1], min_val=1, max_val=MAXR)
            with act.If(rounds > 1):
                with act.Fori(1, rounds) as r:
                    with act.Fori(0, NE) as e:
                        expert_act(act.snap(r * NE + e))
            act.wait_ge(S("moe_sum"), 1)
            for t, (o, n) in enumerate(TILES):
                A(fsq[0:n, t], ht[0:n, t], ACT.Square).then_inc(S("fsq_done"), 1)
            act.wait_ge(S("fss_sum"), 3)
            for t, (o, n) in enumerate(TILES):
                own(A(fss[0:n, t:t + 1], fss[0:n, t:t + 1], ACT.Ln, bias=eps[0:n, 0:1], scale=1.0 / D))
            for t, (o, n) in enumerate(TILES):
                A(fss[0:n, t:t + 1], fss[0:n, t:t + 1], ACT.Exp, scale=-0.5).then_inc(S("frs_done"), 1)

        @block.vector
        def _(dve):
            V = nc.vector
            steps = [0]

            def own(ins):
                steps[0] += 1
                ins.then_inc(S("dve_step"), 1)
                dve.wait_ge(S("dve_step"), steps[0])

            def split_lo(u):
                n = 1408 if PLAN["down", 0] <= u < PLAN["in", 1] else UN
                dve.wait_ge(S("hi_done"), u + 1)
                V.tensor_tensor(spL[:, u % 2, 0:n], raw(u, n), spH[:, u % 2, 0:n].bitcast(F32), ALU.subtract
                                ).then_inc(S("split_done"), 1)

            def norm_t(k, l, which, sqv, src_ready, val, before_rstd=()):
                dve.wait_ge(src_ready, val)
                V.tensor_tensor(sqv[:, 4:8], xT[:, 4:8], xT[:, 4:8], ALU.mult).then_inc(S("sq2_done"), 1)
                for u in before_rstd:
                    split_lo(u)
                dve.wait_ge(S("rstd_done"), k + 1)
                for i in range(KT):
                    ins = V.scalar_tensor_tensor(out=sqv[:, i], in0=xT[:, i],
                                                 scalar=vec[:, l, which * 8 + i:which * 8 + i + 1],
                                                 in1=rstd[:], op0=ALU.mult, op1=ALU.mult)
                    if i % 4 == 3:
                        ins.then_inc(S("hn_f"), 1)
                for half in range(2):
                    dve.wait_ge(S("hnH_done"), 2 * k + half + 1)
                    V.tensor_tensor(hnL[:, 4 * half:4 * half + 4], sqv[:, 4 * half:4 * half + 4],
                                    hnH[:, 4 * half:4 * half + 4].bitcast(F32), ALU.subtract
                                    ).then_inc(S("hnL_done"), 1)

            dve.wait_ge(S("vec_tr"), 1)
            own(V.tensor_copy(vec[:], ps[:, 1, 0:DEPTH * 68].rearrange("p (l n) -> p l n", l=DEPTH)))
            own(V.tensor_tensor(lbt[:, 2], vec[:, 0, 64:68], vec[:, 1, 64:68], ALU.max))
            own(V.tensor_tensor(lbt[:, 0], vec[:, 0, 64:68], lbt[:, 2], ALU.subtract))
            V.tensor_tensor(lbt[:, 1], vec[:, 1, 64:68], lbt[:, 2], ALU.subtract).then_inc(S("lb_max"), 1)
            own(V.memset(lbom[:, 0, 0], 0.0))
            own(V.memset(lbom[:, 0, 1], 1.0))
            own(V.memset(dtb[:], 0.0))

            for l in range(DEPTH):
                u = PLAN["in", l]
                if l == 0:
                    norm_t(0, 0, 0, sq, S("xT_done"), 6, (u, u + 1))
                    dve.wait_ge(S("wn_hi"), 1)
                    V.tensor_tensor(wnL[:], wnr[:], wnH[:].bitcast(F32), ALU.subtract).then_inc(S("wn_lo"), 1)
                    dve.wait_ge(S("lb_exp"), 1)
                    own(V.tensor_tensor(lbt[:, 2], lbt[:, 0], lbt[:, 1], ALU.add))
                    own(V.reciprocal(lbt[:, 3], lbt[:, 2]))
                    own(V.tensor_tensor(lbom[:, 1, 0], lbt[:, 1], lbt[:, 3], ALU.mult))
                    V.tensor_tensor(lbom[:, 1, 1], lbt[:, 0], lbt[:, 3], ALU.mult).then_inc(S("lb_done"), 1)
                else:
                    norm_t(2, 1, 0, sq, S("down_evac"), 8, (u, u + 1))
                dve.wait_ge(S("nar_mm"), l + 1)
                V.tensor_copy(dtT[:], ps[0:NH, 7, 0:TOK]).then_inc(S("nar_done"), 1)
                for c in range(7):
                    split_lo(u + 2 * c + 2)
                    if c == 0:
                        if l:
                            own(V.memset(dtb[:], 0.0))
                        dve.wait_ge(S("dt_mm"), l + 1)
                        own(V.tensor_copy(dtb[:, 0, 0:2], ps[:, 7, 0:16].rearrange("p (t n) -> p t n", t=2)))
                        V.tensor_copy(dtb[0:NS, 0, 2], ps[0:NS, 7, 16:24]).then_inc(S("dt_evac"), 1)
                    split_lo(u + 2 * c + 3)
                    if c == 0:
                        dve.wait_ge(S("dt_evac"), l + 1)
                        dve.wait_ge(S("small_in"), 16 * (4 * DEPTH + 1))
                        own(V.tensor_tensor(dtb[:, 0], dtb[:, 0], bc[:, l, 0].unsqueeze(1).broadcast_to([P, 3, NH]),
                                            ALU.add))
                        V.scalar_tensor_tensor(out=dtb[:, 1], in0=dtb[:, 0], scalar=-1.0, in1=dtb[:, 0],
                                               op0=ALU.mult, op1=ALU.max).then_inc(S("dt_abs"), 1)
                    if c == C_F:
                        dve.wait_ge(S("used"), u + 2 * c + 2)
                        V.tensor_scalar(lfT[:], ps[:, 4:8, 0:TOK], -40.0, None, ALU.max).then_inc(S("fz_done"), 1)
                        dve.wait_ge(S("sigm_done"), l + 1)
                        dve.wait_ge(S("lb_done"), 1)
                        for h in range(H):
                            ins = V.scalar_tensor_tensor(out=kT[:, h], in0=kT[:, h], scalar=lbom[:, l, 1, h:h + 1],
                                                         in1=lfT[:, h], op0=ALU.mult, op1=ALU.mult)
                        ins.then_inc(S("k_done"), 1)
                        dve.wait_ge(S("dt_ln"), l + 1)
                        dve.wait_ge(S("aexp_done"), 1)
                        own(V.scalar_tensor_tensor(out=dtb[:, 3], in0=dtb[:, 0], scalar=0.0, in1=dtb[:, 2],
                                                   op0=ALU.max, op1=ALU.add))
                        V.scalar_tensor_tensor(out=dtb[:, 4], in0=dtb[:, 3], scalar=-1.0,
                                               in1=bc[:, l, 1].unsqueeze(1).broadcast_to([P, 3, NH]),
                                               op0=ALU.mult, op1=ALU.mult).then_inc(S("a_done"), 1)
                    if c in (C_XS, C_BC):
                        dve.wait_ge(S("proj_evac"), 6 * l + c + 1)
                        dve.wait_ge(S("pad_zero"), l + 1)
                        w = PADC - TAPS + 1
                        for k in range(4 * c, 4 * c + 4):
                            if k >= 2:
                                dve.wait_ge(S("conv_done"), 8 * l + k - 1)
                            own(V.tensor_scalar(cvt[:, k % 2, 0:w], xbc[:, k, 0:w], vec[:, l, 24 + k:25 + k],
                                                vec[:, l, 16 + k:17 + k], ALU.mult, ALU.add))
                            for tap in range(1, TAPS):
                                i = V.scalar_tensor_tensor(
                                    out=cvt[:, k % 2, 0:w], in0=xbc[:, k, tap:tap + w],
                                    scalar=vec[:, l, 24 + 8 * tap + k:25 + 8 * tap + k],
                                    in1=cvt[:, k % 2, 0:w], op0=ALU.mult, op1=ALU.add)
                                if tap < TAPS - 1:
                                    own(i)
                                else:
                                    i.then_inc(S("conv_sum"), 1)
                        if c == C_BC:
                            dve.wait_ge(S("cst_tr"), l + 1)
                            own(V.tensor_copy(cpk[:, :, 0:3], xbc[:, :, NPR:NPR + 3]))
                            for k in range(8):
                                V.tensor_copy(cpk[:, k, 3:27].rearrange("p (b r) -> p b r", b=NSQ),
                                              xbc[:, k, 3 + NPR:PADC].rearrange("p (b r) -> p b r", b=NSQ)[:, :, 8:11]
                                              ).then_inc(S("cpk_done"), 1)
                dve.wait_ge(S("tab_in"), 16)
                for t, (o, n) in enumerate(TILES):
                    i = LT(l, t)
                    nl = LV if t < 2 else LS
                    flat = lambda x: x[:].rearrange("p v n -> p (v n)")
                    dve.wait_ge(S("lfH_done"), i + 1)
                    V.tensor_tensor(lfL[0:n], ps[0:n, 4, :], lfH[0:n].bitcast(F32), ALU.subtract
                                    ).then_inc(S("lfL_done"), 1)
                    dve.wait_ge(S("kx_exp"), i + 1)
                    dve.wait_ge(S("k_tr"), i + 1)
                    V.tensor_tensor(kd[0:n], kd[0:n], ps[0:n, 5, :], ALU.mult).then_inc(S("kd_done"), 1)

                    def products(h):
                        j = LTH(l, t, h)
                        Mv = flat(Mb[h % 2])[:, 0:(nl + 1) * n].rearrange("p (v n) -> p v n", n=n)
                        Yqv = flat(Yqb[h % 2])[:, 0:(nl + 1) * n].rearrange("p (v n) -> p v n", n=n)
                        Ykv = flat(Ykb[h % 2])[:, 0:nl * n].rearrange("p (v n) -> p v n", n=n)
                        dve.wait_ge(S("x_exp"), j + 1)
                        if j >= 2:
                            dve.wait_ge(S("o_mm"), j - 1)
                        q_b = qT[:, h, o:o + n].unsqueeze(1).broadcast_to([P, nl + 1, n])
                        k_b = kT[:, h, o:o + n].unsqueeze(1).broadcast_to([P, nl, n])
                        V.tensor_tensor(Yqv, Mv, q_b, ALU.mult)
                        if t < 2:
                            own(V.tensor_copy(egl[:, h, 0:1], Mv[:, nl, n - 1:n]))
                        else:
                            own(V.tensor_copy(egl[:, h], Mv[:, nl, LSQ - 1:n:LSQ]))
                            V.tensor_tensor(qG[:, h], Mv[:, nl], qT[:, h, o:o + n], ALU.mult
                                            ).then_inc(S("qG_done"), 1)
                        V.tensor_tensor(Ykv, Mv[:, 0:nl], k_b, ALU.mult).then_inc(S("y_done2"), 1)

                    products(0)
                    for h in range(H):
                        j = LTH(l, t, h)
                        if h < H - 1:
                            products(h + 1)
                        dve.wait_ge(S("sc_mm"), j + 1)
                        if j >= 2:
                            dve.wait_ge(S("o_mm"), j - 1)
                        SCv = flat(SCb[h % 2])[:, 0:(nl + 1) * n]
                        if t < 2:
                            V.tensor_tensor(SCv, ps[:, 2:4, :].rearrange("p b n -> p (b n)"), tabv("mask"), ALU.mult
                                            ).then_inc(S("sc_done"), 1)
                        else:
                            V.tensor_tensor(SCv[0:n], ps[0:n, 2, 0:(nl + 1) * n], tabv("ms")[0:n], ALU.mult
                                            ).then_inc(S("sc_done"), 1)
                    if t < 2:
                        dve.wait_ge(S("st_mm"), 2 * l + t + 1)
                        if t == 0:
                            if l:
                                dve.wait_ge(S("hgp_stored"), 16 * l)
                            V.tensor_copy(SH[:], ps[:, 7, :]).then_inc(S("sh_done"), 1)
                        else:
                            dve.wait_ge(S("o_mm"), LTH(l, 1, 3) + 1)
                            for h in range(H):
                                c0 = h * P
                                ins = V.scalar_tensor_tensor(out=SH[:, c0:c0 + P], in0=SH[:, c0:c0 + P],
                                                       scalar=egl[:, h, 0:1], in1=ps[:, 7, c0:c0 + P],
                                                       op0=ALU.mult, op1=ALU.add)
                            ins.then_inc(S("sh_done"), 1)
                for b in range(NSQ):
                    dve.wait_ge(S("sst_mm"), l * 8 + b + 1)
                    sv = slab(l, b).rearrange("p (h v) -> p h v", h=H)
                    own(V.tensor_tensor(sv, sv, egl[:, :, b:b + 1].broadcast_to([P, H, P]), ALU.mult))
                    V.tensor_tensor(slab(l, b), slab(l, b), ps[:, 4 + b % 2, :], ALU.add
                                    ).then_inc(S("slab_done"), 1)
                dve.wait_ge(S("o_evac"), LT(l, 2) + 1)
                V.tensor_tensor(oT[:, :, NPR:TOK], oT[:, :, NPR:TOK],
                                ps[:, 3, 0:H * NS].rearrange("p (h n) -> p h n", h=H), ALU.add
                                ).then_inc(S("hg_o"), 1)

                for t, (o, n) in enumerate(TILES):
                    i = LT(l, t)
                    Lt = (tabv("l") if t < 2 else tabv("ls"))[0:n, 0:n]
                    Ut = tabv("w")[:, LV * P:] if t < 2 else tabv("ws")[0:n, LS * n:]
                    av = dtb[0:n, 4, t]
                    if t == 0:
                        dve.wait_ge(S("o_mm"), LTH(l, 2, 3) + 1)
                        dve.wait_ge(S("conv_stored"), 32 * (l + 1))
                    else:
                        dve.wait_ge(S("E_mm"), i)
                        dve.wait_ge(S("yi_mm"), i)
                    V.tensor_tensor(La[0:n, :, 0:n], Lt.unsqueeze(1).broadcast_to([n, NH, n]),
                                    av.unsqueeze(2).broadcast_to([n, NH, n]), ALU.mult).then_inc(S("La_done"), 1)
                    V.tensor_copy(aex[0:n], av.unsqueeze(2).broadcast_to([n, NH, HD])).then_inc(S("aex_done"), 1)
                    if t == 2:
                        V.tensor_tensor(am[0:n], av.unsqueeze(1).broadcast_to([n, NSQ, NH]),
                                        tabv("seq")[0:n].unsqueeze(2).broadcast_to([n, NSQ, NH]), ALU.mult
                                        ).then_inc(S("am_done"), 1)
                    dve.wait_ge(S("xs_tr"), i + 1)
                    if t:
                        dve.wait_ge(S("yi_mm"), i)
                    xv = xdt[0:n].rearrange("p (h d) -> p h d", h=NH)
                    own(V.tensor_tensor(xv, ps[0:n, 4, :].rearrange("p (h d) -> p h d", h=NH),
                                        dtb[0:n, 3, t].unsqueeze(2).broadcast_to([n, NH, HD]), ALU.mult))
                    dve.wait_ge(S("w_exp"), i + 1)
                    V.tensor_tensor(xw[0:n].rearrange("p (h d) -> p h d", h=NH), xv,
                                    wsm[0:n].unsqueeze(2).broadcast_to([n, NH, HD]), ALU.mult
                                    ).then_inc(S("xw_done"), 1)
                    dve.wait_ge(S("cb_mm"), i + 1)
                    own(V.tensor_tensor(CBm[0:n, :, 0:n], ps[0:n, 3, 0:2 * n].rearrange("p (g n) -> p g n", g=G),
                                        Ut.unsqueeze(1).broadcast_to([n, G, n]), ALU.mult))
                    for g in range(G):
                        dve.wait_ge(S("dec_exp"), 2 * i + g + 1)
                        V.tensor_tensor(M[0:n, 4 * g:4 * g + 4, 0:n], M[0:n, 4 * g:4 * g + 4, 0:n],
                                        CBm[0:n, g, 0:n].unsqueeze(1).broadcast_to([n, 4, n]), ALU.mult
                                        ).then_inc(S("P_done"), 1)
                    if t == 2:
                        dve.wait_ge(S("ea_exp"), i + 1)
                        eav = ea[:].rearrange("p (b h) -> p b h", b=NSQ)
                        for b in range(NSQ):
                            if b == 1:
                                dve.wait_ge(S("gsq_done"), 2 * l + 1)
                                V.tensor_tensor(oT[:], oT[:], ogT[:], ALU.mult).then_inc(S("og_done"), 1)
                            if b == 3:
                                dve.wait_ge(S("grs_done"), 2 * l + 1)
                                dve.wait_ge(S("og_done"), l + 1)
                                for h in range(H):
                                    ins = V.scalar_tensor_tensor(out=oT[:, h], in0=oT[:, h],
                                                                 scalar=vec[:, l, 56 + h:57 + h],
                                                                 in1=rsh[:, h], op0=ALU.mult, op1=ALU.mult)
                                ins.then_inc(S("mixed_f"), 1)
                            if b == 5:
                                dve.wait_ge(S("mixH_done"), 2 * l + 1)
                                V.tensor_tensor(hnL[:, 0:4], oT[:], hnH[:, 0:4].bitcast(F32), ALU.subtract
                                                ).then_inc(S("mixL_done"), 1)
                            dve.wait_ge(S("bst_mm"), l * 8 + b + 1)
                            sv = slab(l, 8 + b).rearrange("p (h v) -> p h v", h=NH)
                            own(V.tensor_tensor(sv, sv, eav[:, b].unsqueeze(2).broadcast_to([P, NH, HD]), ALU.mult))
                            V.tensor_tensor(slab(l, 8 + b), slab(l, 8 + b), ps[:, 4 + b % 2, :], ALU.add
                                            ).then_inc(S("slab_done"), 1)
                    if t:
                        dve.wait_ge(S("E_exp"), i + 1)
                        dve.wait_ge(S("yx_mm"), (2 * l + t) if t == 1 else (2 * l + 2))
                        own(V.tensor_tensor(t1[:, :, 0:n], EE[:, :, 0:n],
                                            ps[:, 2, 0:4 * n].rearrange("p (j n) -> p j n", j=4), ALU.mult))
                    dve.wait_ge(S("yi_mm"), i + 1)
                    for j in range(4):
                        for hh in range(2):
                            q0, q1 = hh * HD, (hh + 1) * HD
                            ins = V.scalar_tensor_tensor(
                                out=cvT[q0:q1, j, o:o + n], in0=cvT[q0:q1, j, o:o + n],
                                scalar=bc[q0:q1, l, 2, 2 * j + hh:2 * j + hh + 1],
                                in1=ps[q0:q1, 6, j * n:(j + 1) * n], op0=ALU.mult, op1=ALU.add)
                    if t == 0:
                        ins.then_inc(S("ssd_y"), 1)
                    else:
                        own(ins)
                        V.tensor_tensor(cvT[:, 0:4, o:o + n], cvT[:, 0:4, o:o + n], t1[:, :, 0:n], ALU.add
                                        ).then_inc(S("ssd_y"), 1)
                    if t < 2:
                        dve.wait_ge(S("hst_mm"), 2 * l + t + 1)
                        dve.wait_ge(S("ea_exp"), i + 1)
                        if t == 0:
                            if l:
                                dve.wait_ge(S("ssp_stored"), 16 * l)
                            V.tensor_copy(SS[:], ps[:, 7, :]).then_inc(S("ss_done"), 1)
                        else:
                            sv = SS[:].rearrange("p (h v) -> p h v", h=NH)
                            own(V.tensor_tensor(sv, sv, ea[:, 0:NH].unsqueeze(2).broadcast_to([P, NH, HD]), ALU.mult))
                            V.tensor_tensor(SS[:], SS[:], ps[:, 7, :], ALU.add).then_inc(S("ss_done"), 1)
                dve.wait_ge(S("ssd_y"), 3 * l + 3)
                V.tensor_tensor(cvT[:, 0:4], cvT[:, 0:4], zT[:], ALU.mult).then_inc(S("z_done"), 1)
                dve.wait_ge(S("grs_done"), 2 * l + 2)
                for j in range(4):
                    ins = V.scalar_tensor_tensor(out=cvT[:, j], in0=cvT[:, j], scalar=vec[:, l, 60 + j:61 + j],
                                                 in1=rss[:, j // 2], op0=ALU.mult, op1=ALU.mult)
                ins.then_inc(S("mixed_f"), 1)
                dve.wait_ge(S("mixH_done"), 2 * l + 2)
                V.tensor_tensor(hnL[:, 4:8], cvT[:, 0:4], hnH[:, 4:8].bitcast(F32), ALU.subtract
                                ).then_inc(S("mixL_done"), 1)
                uo = PLAN["out", l]
                for c in range(2):
                    if c == 0:
                        split_lo(uo + 2 * c + 2)
                        split_lo(uo + 2 * c + 3)
                    dve.wait_ge(S("used"), uo + 2 * c + 2)
                    V.tensor_tensor(xT[:, 4 * c:4 * c + 4], xT[:, 4 * c:4 * c + 4], ps[:, 4 * c:4 * c + 4, 0:TOK],
                                    ALU.add).then_inc(S("out_evac"), 1)
                if l == 0:
                    norm_t(1, 0, 1, sq, S("out_evac"), 2, (uo + 4, uo + 5))
                    uu, ud = PLAN["up", 0], PLAN["down", 0]
                    for j in range(11):
                        split_lo(uu + 2 * j + 2)
                        split_lo(uu + 2 * j + 3)
                        bank = 4 * (j % 2) + 2
                        dve.wait_ge(S("gs_done"), j + 1)
                        if j:
                            dve.wait_ge(S("hfH_done"), j)
                            dve.wait_ge(S("hfL_done"), j)
                        V.tensor_tensor(hf[:], gs[:], ps[:, bank:bank + 2, 0:TOK], ALU.mult).then_inc(S("hf_done"), 1)
                        dve.wait_ge(S("hfH_done"), j + 1)
                        V.tensor_tensor(hfL[:, 2 * j:2 * j + 2], hf[:], hfH[:, 2 * j:2 * j + 2].bitcast(F32),
                                        ALU.subtract).then_inc(S("hfL_done"), 1)
                    for m in range(8):
                        if m < 7:
                            split_lo(ud + 2 * m + 2)
                            split_lo(ud + 2 * m + 3)
                        dve.wait_ge(S("used"), ud + 2 * m + 2)
                        V.tensor_tensor(xT[:, m], xT[:, m], ps[:, m, 0:TOK], ALU.add).then_inc(S("down_evac"), 1)

            dve.wait_ge(S("mixer_stored"), 2)
            norm_t(3, 1, 1, sqm, S("out_evac"), 4)
            T = lambda k: sml[:, k]
            one = lambda v: v[:, :, 0:1].broadcast_to([P, 3, NE])
            dve.wait_ge(S("nar_mm"), 3)
            V.tensor_copy(sg[0:NE, 1, 0:TOK], ps[0:NE, 1, 0:TOK]).then_inc(S("nar_done"), 1)
            own(V.memset(T(0), 0.0))
            dve.wait_ge(S("lg_mm"), 1)
            own(V.tensor_copy(sml[:, 0, 0:2], ps[:, 1, 0:16].rearrange("p (t n) -> p t n", t=2)))
            own(V.tensor_copy(sml[0:NS, 0, 2], ps[0:NS, 1, 16:24]))
            io8 = tabv("iota")[:, 0:NE].unsqueeze(1).broadcast_to([P, 3, NE])

            def choose(src, top, hot):
                own(V.tensor_reduce(sml[:, top, :, 0:1], T(src), AX.X, ALU.max))
                own(V.tensor_tensor(T(hot), T(src), one(T(top)), ALU.is_equal))
                own(V.tensor_scalar(T(hot), T(hot), -100.0, 100.0, ALU.mult, ALU.add))
                own(V.tensor_tensor(T(hot), T(hot), io8, ALU.add))
                own(V.tensor_reduce(sml[:, 10, :, 0:1], T(hot), AX.X, ALU.min))
                own(V.tensor_tensor(T(hot), io8, one(T(10)), ALU.is_equal))

            choose(0, 1, 2)
            own(V.tensor_scalar(T(3), T(2), -1.0, 1.0, ALU.mult, ALU.add))
            own(V.tensor_tensor(T(3), T(3), T(0), ALU.mult))
            own(V.tensor_scalar(T(4), T(2), -3.0e38, None, ALU.mult))
            own(V.tensor_tensor(T(3), T(3), T(4), ALU.add))
            choose(3, 5, 6)
            V.tensor_tensor(sml[:, 8, :, 0:1], sml[:, 5, :, 0:1], sml[:, 1, :, 0:1], ALU.subtract
                            ).then_inc(S("rt_diff"), 1)
            V.tensor_tensor(T(7), T(2), T(6), ALU.add).then_inc(S("routed"), 1)
            dve.wait_ge(S("rt_exp"), 1)
            own(V.tensor_scalar(sml[:, 11, :, 0:1], sml[:, 9, :, 0:1], 1.0, None, ALU.add))
            own(V.reciprocal(sml[:, 8, :, 0:1], sml[:, 11, :, 0:1]))
            own(V.tensor_tensor(sml[:, 9, :, 0:1], sml[:, 9, :, 0:1], sml[:, 8, :, 0:1], ALU.mult))
            own(V.tensor_tensor(T(2), T(2), one(T(8)), ALU.mult))
            own(V.tensor_tensor(T(6), T(6), one(T(9)), ALU.mult))
            own(V.tensor_tensor(gate[:].rearrange("p e t -> p t e"), T(2), T(6), ALU.add))
            dve.wait_ge(S("routed"), 1)
            dve.wait_ge(S("rank_mm"), 1)
            own(V.memset(T(3), 0.0))
            own(V.tensor_scalar(sml[:, 3, 0:2], ps[:, 1, 32:48].rearrange("p (t n) -> p t n", t=2), 1.0, None, ALU.add))
            own(V.tensor_scalar(sml[0:NS, 3, 2], ps[0:NS, 1, 48:56], 1.0, None, ALU.add))
            own(V.tensor_tensor(T(3), T(3), T(7), ALU.mult))
            own(V.tensor_scalar(rank[:, 0:NE].rearrange("p e t -> p t e"), T(3), -1.0, None, ALU.add))
            own(V.tensor_scalar(rank[:, NE], rank[:, 0], -float(CAP), None, ALU.add))
            own(V.tensor_reduce(rnd[:, 0:1], ps[:, 1, 64:72], AX.X, ALU.max))
            own(V.tensor_scalar(rnd[:, 1:2], rnd[:, 0:1], float(CAP), 1.0, ALU.is_gt, ALU.add))
            for k in range(2, MAXR):
                own(V.tensor_scalar(rnd[:, 2:3], rnd[:, 0:1], float(CAP * k), None, ALU.is_gt))
                own(V.tensor_tensor(rnd[:, 1:2], rnd[:, 1:2], rnd[:, 2:3], ALU.add))
            V.tensor_copy(rndi[:], rnd[:, 1:2]).then_inc(S("rounds_ready"), 1)

            own(V.memset(selT[:].bitcast(F32), 0.0))
            dve.sem_inc(S("eh_done"), 1)
            V.memset(rk[:, 1], 0.0).then_inc(S("rk_done"), 1)
            V.memset(yH[:].bitcast(F32), 0.0).then_inc(S("yL_done"), 1)
            V.memset(yL[:].bitcast(F32), 0.0).then_inc(S("yL_done"), 1)

            def expert_lo(it, j):
                dve.wait_ge(S("hi_done"), it * EU + (U0 + j + 1))
                hi, lo = esplit(j)
                V.tensor_tensor(lo, eslot(j)[0], hi.bitcast(F32), ALU.subtract).then_inc(S("split_done"), 1)

            def one_hot(ranks):
                for t in range(3):
                    i = V.tensor_scalar(sel[:, t], tabv("iota"), ranks[:, t:t + 1], None, ALU.is_equal)
                i.then_inc(S("sel_done"), 1)

            def gathered_lo(it):
                for q in range(2):
                    dve.wait_ge(S("X_done"), it * 2 + (q + 1))
                    V.tensor_tensor(XL[:, 4 * q:4 * q + 4], ps[:, 2 + q, :].rearrange("p (k n) -> p k n", k=4),
                                    XH[:, 4 * q:4 * q + 4].bitcast(F32), ALU.subtract).then_inc(S("XL_done"), 1)

            def scatter_add(it, t):
                n = TILES[t][1]
                for q in range(2):
                    dve.wait_ge(S("scat_mm"), it * 6 + (2 * t + q + 1))
                    V.scalar_tensor_tensor(out=ht[0:n, t, 512 * q:512 * q + 512], in0=ps[0:n, 2 + 2 * t + q, :],
                                           scalar=rk[0:n, 1, t:t + 1], in1=ht[0:n, t, 512 * q:512 * q + 512],
                                           op0=ALU.mult, op1=ALU.add).then_inc(S("ht_add"), 1)

            def expert_dve(e, it):
                nxt = dve.snap(e + 1)
                for p in range(EU):
                    if p == 6:
                        dve.wait_ge(S("selT_tr"), it + 1)
                        V.tensor_copy(selT[:].rearrange("p t n -> p (t n)")[:, 0:TOK], ps[:, 5, 0:TOK]
                                      ).then_inc(S("selT_done"), 1)
                        V.tensor_copy(rk[:, 0], rank[:, bass.ds(nxt, 1), :].rearrange("p e t -> p (e t)")
                                      ).then_inc(S("rk_done"), 1)
                        dve.wait_ge(S("rk_done"), it * 2 + 2)
                        one_hot(rk[:, 0])
                    if p in UP_LAST:
                        c = UP_LAST.index(p)
                        dve.wait_ge(S("sg_done"), it * EC + (c + 1))
                        if c:
                            dve.wait_ge(S("eh_tr"), it * EC + c)
                        V.tensor_tensor(sg[:, 1], sg[:, 0], ps[:, 2 * (c % 2) + 1, :], ALU.mult
                                        ).then_inc(S("eh_done"), 1)
                    if p in TURN_AT:
                        c = TURN_AT.index(p)
                        dve.wait_ge(S("hTH_done"), it * EC + (c + 1))
                        V.tensor_tensor(hTL[:], ps[:, 4, :].rearrange("p (k n) -> p k n", k=4), hTH[:].bitcast(F32),
                                        ALU.subtract).then_inc(S("hTL_done"), 1)
                    expert_lo(it, p + AHEAD)
                    if p == 2:
                        dve.wait_ge(S("rk_done"), it * 2 + 1)
                    if 2 <= p < 5:
                        scatter_add(it, p - 2)
                    if p == UP_LAST[-1]:
                        gathered_lo(it + 1)
                V.tensor_copy(rk[:, 1], gate[:, bass.ds(e, 1), :].rearrange("p e t -> p (e t)")).then_inc(S("rk_done"), 1)
                for q in range(2):
                    dve.wait_ge(S("yH_done"), it * 2 + (q + 1))
                    V.tensor_tensor(yL[:, 512 * q:512 * q + 512], ps[:, 6 + q, :],
                                    yH[:, 512 * q:512 * q + 512].bitcast(F32), ALU.subtract).then_inc(S("yL_done"), 1)

            one_hot(rank[:, 0])
            for j in range(AHEAD):
                expert_lo(0, j)
            gathered_lo(0)
            with dve.Fori(0, NE) as e:
                expert_dve(e, e)
            rounds = dve.value_load(rndi[0:1, 0:1], min_val=1, max_val=MAXR)
            with dve.If(rounds > 1):
                with dve.Fori(1, rounds) as r:
                    V.tensor_scalar(rank[:], rank[:], -float(CAP), None, ALU.add)
                    dve.drain()
                    with dve.Fori(0, NE) as e:
                        expert_dve(e, dve.snap(r * NE + e))
            last = dve.snap(rounds * NE)
            dve.wait_ge(S("rk_done"), last * 2 + 1)
            for t in range(3):
                scatter_add(last, t)
            dve.drain().then_inc(S("moe_sum"), 1)
            for t, (o, n) in enumerate(TILES):
                dve.wait_ge(S("fsq_done"), t + 1)
                V.tensor_reduce(fss[0:n, t:t + 1], fsq[0:n, t], AX.X, ALU.add).then_inc(S("fss_sum"), 1)
            dve.wait_ge(S("gfin_in"), 16)
            for t, (o, n) in enumerate(TILES):
                dve.wait_ge(S("frs_done"), t + 1)
                V.scalar_tensor_tensor(out=ht[0:n, t], in0=ht[0:n, t], scalar=fss[0:n, t:t + 1], in1=gfin[0:n],
                                       op0=ALU.mult, op1=ALU.mult).then_inc(S("y_done"), 1)

        @block.tensor
        def _(pe):
            mm = nc.tensor.matmul

            def three(out, lhs, rhs, start, stop):
                mm(out, lhs[0], rhs[0], start=start, stop=False)
                mm(out, lhs[0], rhs[1], start=False, stop=False)
                return mm(out, lhs[1], rhs[0], start=False, stop=stop)

            def unit(u, k):
                n = 1408 if PLAN["down", 0] <= u < PLAN["in", 1] else UN
                return [x[:, u % 2, 0:n].rearrange("p (k n) -> p k n", k=k) for x in (spH, spL)]

            def norm_mm(k, sqv):
                for i in range(KT):
                    if i % 4 == 0:
                        pe.wait_ge(S("sq_done") if i == 0 else S("sq2_done"), k + 1)
                    m = mm(ps[:, 0, 0:TOK], onesf, sqv[:, i], start=i == 0, stop=i == KT - 1)
                m.then_inc(S("ss_mm"), 1)

            def narrow(k, out, before):
                pe.wait_ge(S("wn_lo"), 1)
                for i in range(KT):
                    if i % 4 == 0:
                        pe.wait_ge(S("hnL_done"), before + 1 + i // 4)
                    m = three(out[0:NH, 0:TOK], (wnH[:, k, i], wnL[:, k, i]), (hnH[:, i], hnL[:, i]),
                              start=i == 0, stop=i == KT - 1)
                m.then_inc(S("nar_mm"), 1)

            def narrow_turn(k, src, out):
                pe.wait_ge(S("nar_done"), k + 1)
                for t, (o, n) in enumerate(TILES):
                    m = nc.tensor.transpose(out[0:n, 8 * t:8 * t + 8], src[:, o:o + n], ident[0:NH, 0:NH])
                return m

            pe.wait_ge(S("id_in"), 16)
            pe.wait_ge(S("x_in"), 48)
            for t, (o, n) in enumerate(TILES):
                for half in range(2):
                    i = 2 * t + half
                    if i >= 2:
                        pe.wait_ge(S("xT_done"), i - 1)
                    for k in range(4):
                        m = nc.tensor.transpose(ps[:, 2 + i % 2, k * n:(k + 1) * n],
                                                xin[0:n, t, (4 * half + k) * P:(4 * half + k + 1) * P],
                                                ident[0:n, 0:n])
                    m.then_inc(S("xin_tr"), 1)
            for l in range(DEPTH):
                pe.wait_ge(S(f"vec_in{l}"), 16 * 7)
                m = nc.tensor.transpose(ps[:, 1, 68 * l:68 * l + 68], vin[:, l], ident[0:68, 0:68])
            m.then_inc(S("vec_tr"), 1)

            for l in range(DEPTH):
                norm_mm(2 * l, sq)
                pe.wait_ge(S("cst_in"), 16 * (l + 1))
                for k in range(8):
                    m = nc.tensor.transpose(ps[:, 6, 24 * k:24 * k + 24], cst[:, k * P:(k + 1) * P], ident[0:24, 0:24])
                m.then_inc(S("cst_tr"), 1)
                narrow(l, ps[:, 7], 4 * l)

                def dense(u, c, inputs=None):
                    for half in range(2):
                        if inputs:
                            pe.wait_ge(inputs[0], inputs[1] + half + 1)
                        pe.wait_ge(S("split_done"), u + half + 1)
                        wH, wL = unit(u + half, 4)
                        for i in range(4):
                            for k in range(4):
                                kk = 4 * half + k
                                m = three(ps[:, 4 * (c % 2) + i, 0:TOK],
                                          (wH[:, k, i * P:(i + 1) * P], wL[:, k, i * P:(i + 1) * P]),
                                          (hnH[:, kk], hnL[:, kk]), start=kk == 0, stop=kk == KT - 1)
                        if half == 0:
                            m.then_inc(S("used"), 1)
                    return m

                for c in range(7):
                    if c == 0:
                        pe.wait_ge(S("rstd_done"), 2 * l + 1)
                    if c == 1:
                        pe.wait_ge(S("pads_done"), 8 * (l + 1))
                        pe.wait_ge(S("dt_evac"), l + 1)
                    if c >= 2:
                        pe.wait_ge(S("proj_evac"), 6 * l + c - 1)
                    dense(PLAN["in", l] + 2 * c, c).then_inc(S("used"), 1)
                    if c == 0:
                        narrow_turn(l, dtT, ps[:, 7]).then_inc(S("dt_mm"), 1)

                pe.wait_ge(S("cpk_done"), 8 * (l + 1))
                pe.wait_ge(S("proj_evac"), 6 * (l + 1))
                for half in range(2):
                    for k in range(4):
                        m = nc.tensor.transpose(ps[0:27, 2 + half, k * P:(k + 1) * P], cpk[:, 4 * half + k, :], ident)
                    m.then_inc(S("cso_tr"), 1)

                for t, (o, n) in enumerate(TILES):
                    i = LT(l, t)
                    nl = LV if t < 2 else LS
                    pe.wait_ge(S("lf_done"), H * (l + 1))
                    pe.wait_ge(S("tab_round"), 1)
                    if t:
                        pe.wait_ge(S("v_done"), i)
                    for h in range(H):
                        m = nc.tensor.transpose(ps[0:n, 4, h * P:(h + 1) * P], lfT[:, h, o:o + n], ident)
                    m.then_inc(S("lf_tr"), 1)
                    if t:
                        pe.wait_ge(S("kd_done"), i)
                    for h in range(H):
                        m = nc.tensor.transpose(ps[0:n, 5, h * P:(h + 1) * P], kT[:, h, o:o + n], ident)
                    m.then_inc(S("k_tr"), 1)
                    pe.wait_ge(S("lfL_done"), i + 1)
                    if t:
                        pe.wait_ge(S("sh_done"), 2 * l + t)
                    Lr = tabv("l", F32R) if t < 2 else tabv("ls", F32R)[0:n]
                    mm(ps[:, 7, :], Lr, lfH[0:n], start=True, stop=False)
                    mm(ps[:, 7, :], Lr, lfL[0:n], start=False, stop=True).then_inc(S("kx_mm"), 1)
                    for h in range(H):
                        m = nc.tensor.transpose(ps[0:n, 4, h * P:(h + 1) * P], oT[:, h, o:o + n], ident)
                    m.then_inc(S("v_tr"), 1)

                    def exponents(h):
                        j = LTH(l, t, h)
                        if h or t:
                            pe.wait_ge(S("x_exp"), j)
                        W = tabv("w", F32R) if t < 2 else tabv("ws", F32R)[0:n]
                        for b in range(2 if t < 2 else 1):
                            w = W[:, 512 * b:512 * b + 512] if t < 2 else W
                            out = ps[:, b, 0:w.shape[1]]
                            mm(out, lfH[0:n, h * P:(h + 1) * P], w, start=True, stop=False)
                            m = mm(out, lfL[0:n, h * P:(h + 1) * P], w, start=False, stop=True)
                        m.then_inc(S("x_mm"), 1)

                    flat = lambda x: x[:].rearrange("p v n -> p (v n)")

                    def scores(h):
                        j = LTH(l, t, h)
                        pe.wait_ge(S("y_done2"), j + 1)
                        if j == LTH(l, 0, 0):
                            pe.wait_ge(S("cso_done"), 2 * l + 2)
                        if j:
                            pe.wait_ge(S("sc_done"), j)
                        for v in range(nl + 1):
                            out = ps[0:n, 2 + (v * n) // 512, (v * n) % 512:(v * n) % 512 + n]
                            if v < nl:
                                m = mm(out, flat(Ykb[h % 2])[:, v * n:(v + 1) * n],
                                       flat(Yqb[h % 2])[:, v * n:(v + 1) * n], start=True, stop=True)
                            else:
                                m = mm(out, kT[:, h, o:o + n], qT[:, h, o:o + n], start=True, stop=True)
                        m.then_inc(S("sc_mm"), 1)

                    def output(h):
                        pe.wait_ge(S("sc_done"), LTH(l, t, h) + 1)
                        pe.wait_ge(S("v_done"), i + 1)
                        if h == 0 and t:
                            pe.wait_ge(S("o_evac"), i)
                        out = ps[:, 6, h * n:(h + 1) * n]
                        for v in range(nl + 1):
                            m = mm(out, vtk[0:n, h * P:(h + 1) * P], flat(SCb[h % 2])[0:n, v * n:(v + 1) * n],
                                   start=v == 0, stop=v == nl and t != 1)
                        if t == 1:
                            if h == 0:
                                pe.wait_ge(S("sh_done"), 2 * l + 1)
                            m = mm(out, SH[:, h * P:(h + 1) * P], flat(Yqb[h % 2])[:, nl * n:(nl + 1) * n],
                                   start=False, stop=True)
                        m.then_inc(S("o_mm"), 1)

                    exponents(0)
                    for h in range(H):
                        if h < H - 1:
                            exponents(h + 1)
                        if h:
                            output(h - 1)
                        scores(h)
                    output(H - 1)
                    if t < 2:
                        pe.wait_ge(S("kd_done"), i + 1)
                        for h in range(H):
                            m = mm(ps[:, 7, h * P:(h + 1) * P], kd[0:n, h * P:(h + 1) * P],
                                   vtk[0:n, h * P:(h + 1) * P], start=True, stop=True)
                        m.then_inc(S("st_mm"), 1)
                pe.wait_ge(S("qG_done"), H * (l + 1))
                pe.wait_ge(S("kd_done"), LT(l, 2) + 1)
                for b in range(NSQ):
                    pe.wait_ge(slab_in[b // 4], 16 * 4 * (l + 1))
                    for h in range(H):
                        mm(ps[:, 3, h * NS + b * LSQ:h * NS + (b + 1) * LSQ], slab(l, b)[:, h * P:(h + 1) * P],
                           qG[:, h, b * LSQ:(b + 1) * LSQ], start=True, stop=True)
                    pe.wait_ge(S("kdm_done"), 8 * l + b + 1)
                    if b >= 2:
                        pe.wait_ge(S("slab_done"), 16 * l + b - 1)
                    for h in range(H):
                        m = mm(ps[:, 4 + b % 2, h * P:(h + 1) * P], kdm[:, b % 4, h * P:(h + 1) * P],
                               vtk[0:NS, h * P:(h + 1) * P], start=True, stop=True)
                    m.then_inc(S("sst_mm"), 1)

                for t, (o, n) in enumerate(TILES):
                    i = LT(l, t)
                    Lf = (tabv("l") if t < 2 else tabv("ls"))[0:n, 0:n]
                    Uf = tabv("w")[:, LV * P:] if t < 2 else tabv("ws")[0:n, LS * n:]
                    if t == 0:
                        pe.wait_ge(S("slab_done"), 16 * l + 8)
                        pe.wait_ge(S("conv_done"), 8 * (l + 1))
                    else:
                        pe.wait_ge(S("xw_done"), i)
                        pe.wait_ge(S("Bt_done"), i)
                    for j in range(4):
                        m = nc.tensor.transpose(ps[0:n, 4, j * P:(j + 1) * P], cvT[:, j, o:o + n], ident)
                    m.then_inc(S("xs_tr"), 1)
                    for g in range(G):
                        m = nc.tensor.transpose(ps[0:n, 5, g * P:(g + 1) * P], cvT[:, 4 + g, o:o + n], ident)
                    pe.wait_ge(S("a_done"), l + 1)
                    mm(ps[0:n, 5, 256:264], Lf, dtb[0:n, 4, t], start=True, stop=True)
                    if t < 2:
                        m = mm(ps[:, 5, 264:272], onesf, dtb[:, 4, t], start=True, stop=True)
                    else:
                        pe.wait_ge(S("am_done"), l + 1)
                        m = mm(ps[:, 5, 264:264 + NSQ * NH], onesf[0:n], am[0:n].rearrange("p b h -> p (b h)"),
                               start=True, stop=True)
                    m.then_inc(S("w_mm"), 1)
                    pe.wait_ge(S("La_done"), i + 1)
                    if t:
                        pe.wait_ge(S("dec_exp"), 2 * i)
                    for r in range(NH):
                        m = mm(ps[0:n, r // 4, (r % 4) * n:(r % 4 + 1) * n], La[0:n, r, 0:n], Uf, start=True, stop=True)
                    m.then_inc(S("diff_mm"), 1)
                    pe.wait_ge(S("aex_done"), i + 1)
                    if t == 0:
                        pe.wait_ge(S("hg_o"), l + 1)
                        pe.wait_ge(S("sc_done"), LTH(l, 2, 3) + 1)
                    else:
                        pe.wait_ge(S("ssd_y"), i)
                        pe.wait_ge(S("E_exp"), i)
                    for j in range(4):
                        m = mm(ps[:, 2, j * n:(j + 1) * n], aex[0:n, 2 * j:2 * j + 2, :].rearrange("p h d -> p (h d)"), Uf,
                               start=True, stop=True)
                    m.then_inc(S("E_mm"), 1)
                    if t:
                        pe.wait_ge(S("P_done"), 2 * i)
                    for g in range(G):
                        m = mm(ps[0:n, 3, g * n:(g + 1) * n], cvT[:, 4 + g, o:o + n], cvT[:, 6 + g, o:o + n],
                               start=True, stop=True)
                    m.then_inc(S("cb_mm"), 1)
                    if t == 1:
                        pe.wait_ge(S("E_exp"), i + 1)
                        pe.wait_ge(S("ss_done"), 2 * l + 1)
                        for j in range(4):
                            m = mm(ps[:, 2, j * n:(j + 1) * n], SS[:, j * P:(j + 1) * P], cvT[:, 6 + j // 2, o:o + n],
                                   start=True, stop=True)
                        m.then_inc(S("yx_mm"), 1)
                    pe.wait_ge(S("xw_done"), i + 1)
                    pe.wait_ge(S("P_done"), 2 * i + 2)
                    if t == 0:
                        pe.wait_ge(S("o_evac"), LT(l, 2) + 1)
                    for j in range(4):
                        for hh in range(2):
                            r = 2 * j + hh
                            m = mm(ps[hh * HD:(hh + 1) * HD, 6, j * n:(j + 1) * n], xdt[0:n, r * HD:(r + 1) * HD],
                                   M[0:n, r, 0:n], start=True, stop=True)
                    m.then_inc(S("yi_mm"), 1)
                    if t < 2:
                        pe.wait_ge(S("Bt_done"), i + 1)
                        if t == 0:
                            pe.wait_ge(S("kx_exp"), LT(l, 2) + 1)
                        else:
                            pe.wait_ge(S("ss_done"), 2 * l + t)
                        for g in range(G):
                            m = mm(ps[:, 7, 256 * g:256 * g + 256], Bt[0:n, g * P:(g + 1) * P],
                                   xw[0:n, 256 * g:256 * g + 256], start=True, stop=True)
                        m.then_inc(S("hst_mm"), 1)
                pe.wait_ge(S("gsq_done"), 2 * l + 1)
                pe.wait_ge(S("ss_done"), 2 * l + 2)
                for h, bank in enumerate(HG_BANKS):
                    m = mm(ps[:, bank, 0:TOK], onesf, sqh[:, h], start=True, stop=True)
                m.then_inc(S("gss_mm"), 1)
                pe.wait_ge(S("E_exp"), LT(l, 2) + 1)
                for b in range(NSQ):
                    pe.wait_ge(slab_in[2 + b // 4], 16 * 4 * (l + 1))
                    for j in range(4):
                        m = mm(ps[:, 2, j * NS + b * LSQ:j * NS + (b + 1) * LSQ], slab(l, 8 + b)[:, j * P:(j + 1) * P],
                               cvT[:, 6 + j // 2, NPR + b * LSQ:NPR + (b + 1) * LSQ], start=True, stop=True)
                    if b == NSQ - 1:
                        m.then_inc(S("yx_mm"), 1)
                    pe.wait_ge(S("Bm_done"), 8 * l + b + 1)
                    if b >= 2:
                        pe.wait_ge(S("slab_done"), 16 * l + 8 + b - 1)
                    elif b == 0:
                        pe.wait_ge(S("Bt_done"), LT(l, 2) + 1)
                    for g in range(G):
                        m = mm(ps[:, 4 + b % 2, 256 * g:256 * g + 256], Bm[:, b, g * P:(g + 1) * P],
                               xw[0:NS, 256 * g:256 * g + 256], start=True, stop=True)
                    m.then_inc(S("bst_mm"), 1)

                pe.wait_ge(S("gsq_done"), 2 * l + 2)
                pe.wait_ge(S("slab_done"), 16 * l + 16)
                for j in range(4):
                    m = mm(ps[:, 4 + j // 2, 0:TOK], onesf, sqs[:, j], start=j % 2 == 0, stop=j % 2 == 1)
                m.then_inc(S("gss_mm"), 1)
                for c in range(2):
                    dense(PLAN["out", l] + 2 * c, c, (S("mixL_done"), 2 * l) if c == 0 else None
                          ).then_inc(S("used"), 1)

                if l == 0:
                    norm_mm(1, sq)
                    for j in range(11):
                        for half in range(2):
                            u = PLAN["up", 0] + 2 * j + half
                            pe.wait_ge(S("split_done"), u + 1)
                            if j >= 2 and half == 0:
                                pe.wait_ge(S("hf_done"), j - 1)
                            wH, wL = unit(u, 8)
                            for i in range(2):
                                for k in range(KT):
                                    if j == half == i == 0 and k % 4 == 0:
                                        pe.wait_ge(S("hnL_done"), 2 + 1 + k // 4)
                                    if j == half == i == 0 and k == 0:
                                        pe.wait_ge(S("rstd_done"), 2)
                                    m = three(ps[:, 4 * (j % 2) + 2 * half + i, 0:TOK],
                                              (wH[:, k, i * P:(i + 1) * P], wL[:, k, i * P:(i + 1) * P]),
                                              (hnH[:, k], hnL[:, k]), start=k == 0, stop=k == KT - 1)
                            m.then_inc(S("used"), 1)
                    pe.wait_ge(S("hfL_done"), 11)
                    for m_ in range(8):
                        for half in range(2):
                            u = PLAN["down", 0] + 2 * m_ + half
                            pe.wait_ge(S("split_done"), u + 1)
                            wH, wL = unit(u, 11)
                            for k in range(11):
                                kk = 11 * half + k
                                m = three(ps[:, m_, 0:TOK], (wH[:, k], wL[:, k]), (hfH[:, kk], hfL[:, kk]),
                                          start=kk == 0, stop=kk == 21)
                            m.then_inc(S("used"), 1)

            pe.wait_ge(S("out_evac"), 4)
            norm_mm(3, sqm)
            narrow(2, ps[:, 1], 6)
            m = narrow_turn(2, sg[0:NE, 1], ps[:, 1])
            m.then_inc(S("lg_mm"), 1)
            for t, (o, n) in enumerate(TILES):
                for q in range(4):
                    k = 4 * t + q
                    if k >= 2:
                        pe.wait_ge(S("tk_done"), k - 1)
                    src = sqm if q < 2 else xT
                    for i in range(4):
                        m = nc.tensor.transpose(ps[0:n, 4 + k % 2, i * P:(i + 1) * P], src[:, 4 * (q % 2) + i, o:o + n], ident)
                    m.then_inc(S("tk_tr"), 1)
            pe.wait_ge(S("routed"), 1)
            for t, (o, n) in enumerate(TILES):
                for tt in range(t + 1):
                    nn = TILES[tt][1]
                    w = tabv("before")[0:nn, 0:n] if tt == t else onesf[0:nn, 0:n]
                    mm(ps[0:n, 1, 32 + 8 * t:40 + 8 * t], w, sml[0:nn, 7, tt], start=tt == 0, stop=tt == t)
            for tt in range(3):
                nn = TILES[tt][1]
                m = mm(ps[:, 1, 64:72], onesf[0:nn], sml[0:nn, 7, tt], start=tt == 0, stop=tt == 2)
            m.then_inc(S("rank_mm"), 1)
            pe.wait_ge(S("rounds_ready"), 1)
            pe.wait_ge(S("tk_done"), 12)

            def gather(it):
                pe.wait_ge(S("sel_done"), it + 1)
                for q in range(2):
                    for k in range(4):
                        kk = 4 * q + k
                        for t, (o, n) in enumerate(TILES):
                            m = mm(ps[:, 2 + q, k * P:(k + 1) * P], hk[0:n, t, kk * P:(kk + 1) * P],
                                   sel[0:n, t].bitcast(F32), start=t == 0, stop=t == 2)
                    m.then_inc(S("gath_mm"), 1)

            def scatter(it):
                pe.wait_ge(S("yL_done"), it * 2 + 2)
                for t in range(3):
                    for q in range(2):
                        mm(ps[:, 2 + 2 * t + q, :], selT[:, t], yH[:, 512 * q:512 * q + 512], start=True, stop=False)
                        mm(ps[:, 2 + 2 * t + q, :], selT[:, t], yL[:, 512 * q:512 * q + 512], start=False, stop=True
                           ).then_inc(S("scat_mm"), 1)

            def expert_pe(it):
                pe.wait_ge(S("XL_done"), it * 2 + 2)
                for j, (kind, c, i) in enumerate(EXPERT_UNITS):
                    if j == 2:
                        scatter(it)
                    if j == 4:
                        pe.wait_ge(S("ht_add"), it * 6 + 2)
                    pe.wait_ge(S("split_done"), it * EU + (U0 + j + 1))
                    wH, wL = [x.rearrange("p (k n) -> p k n", k=4 if kind == "up" else 2) for x in esplit(j)]
                    if kind == "up":
                        if i == 0 and c >= 2:
                            pe.wait_ge(S("eh_done"), it * EC + c)
                        for k in range(4):
                            kk = 4 * (i % 2) + k
                            m = three(ps[:, 2 * (c % 2) + i // 2, :], (XH[:, kk], XL[:, kk]), (wH[:, k], wL[:, k]),
                                      start=kk == 0, stop=kk == KT - 1)
                    else:
                        if i == 0:
                            pe.wait_ge(S("hTL_done"), it * EC + (c + 1))
                        for k in range(2):
                            f = 2 * i + k
                            for q in range(2):
                                m = three(ps[:, 6 + q, :], (hTH[:, f], hTL[:, f]),
                                          (wH[:, k, 512 * q:512 * q + 512], wL[:, k, 512 * q:512 * q + 512]),
                                          start=c == 0 and f == 0, stop=c == EC - 1 and f == 3)
                    m.then_inc(S("used"), 1)
                    if j == 5:
                        pe.wait_ge(S("ht_add"), it * 6 + 6)
                        for t, (o, n) in enumerate(TILES):
                            m = nc.tensor.transpose(ps[:, 5, o:o + n], sel[0:n, t].bitcast(F32), ident[0:n, 0:n])
                        m.then_inc(S("selT_tr"), 1)
                    if j == UP_LAST[-1]:
                        pe.wait_ge(S("eh_done"), it * EC + EC)
                        gather(it + 1)
                    if j in TURN_AT:
                        c = TURN_AT.index(j)
                        pe.wait_ge(S("eh_done"), it * EC + (c + 2))
                        if c:
                            pe.wait_ge(S("hTL_done"), it * EC + c)
                        for k in range(4):
                            m = nc.tensor.transpose(ps[:, 4, k * P:(k + 1) * P], sg[:, 1, k * P:(k + 1) * P], ident)
                        m.then_inc(S("eh_tr"), 1)

            gather(0)
            with pe.Fori(0, NE) as e:
                expert_pe(e)
            rounds = pe.value_load(rndi[0:1, 0:1], min_val=1, max_val=MAXR)
            with pe.If(rounds > 1):
                with pe.Fori(1, rounds) as r:
                    with pe.Fori(0, NE) as e:
                        expert_pe(pe.snap(r * NE + e))
            scatter(pe.snap(rounds * NE))


_INS = ["x_prompt", "x_sample", "state_hgrn", "state_ssm", "state_conv", "norm_mix", "w_in", "conv_w", "conv_b",
        "a_log", "dt_bias", "d_skip", "lb_param", "hg_norm", "ssd_norm", "w_out", "norm_ffn", "w_ffn_in",
        "w_ffn_out", "w_router", "w_exp_in", "w_exp_out", "norm_final"]
_OUTS = [(1, NPR, D), (NSQ, LSQ, D), (DEPTH, 1, H, P, P), (DEPTH, 1, NH, P, HD), (DEPTH, 1, 3, CONV),
         (DEPTH, NSQ, H, P, P), (DEPTH, NSQ, NH, P, HD), (DEPTH, NSQ, 3, CONV)]


def kernel(**inputs):
    import concourse.bacc as _bacc
    from concourse.bass_utils import run_bass_kernel_spmd as _run

    nc = _bacc.Bacc("TRN2", target_bir_lowering=False, num_devices=1)
    arrays, aps = {}, {}
    table, at = constants()
    for name in _INS + ["table"]:
        arr = np.ascontiguousarray(table if name == "table" else inputs[name])
        arrays[f"in_{name}_dram"] = arr
        aps[name] = nc.dram_tensor(f"in_{name}_dram", arr.shape, mybir.dt.from_np(arr.dtype),
                                   kind="ExternalInput").ap()
    outs = [nc.dram_tensor(f"out_{i}_dram", shape, F32, kind="ExternalOutput").ap() for i, shape in enumerate(_OUTS)]
    build(nc, aps, outs, table, at)
    r = _run(nc, [arrays], core_ids=[0])
    return tuple(r.results[0][f"out_{i}_dram"] for i in range(len(_OUTS)))
```
